# Optimizing a Trainium2 kernel written in Bass

```python
import jax, jax.numpy as jnp
from jax import lax
import numpy as np

D_MODEL = 1024
BATCH = 1
SEQ = 256
DEPTH = 2

HEAD_DIM = 64
FOX_HEADS = 6
DIL_KV_HEADS = 4
DIL_PATTERNS = ((128, 1), (512, 4), (2048, 16))
DIL_Q_HEADS = DIL_KV_HEADS * len(DIL_PATTERNS)
MOBA_HEADS = 6
MOBA_BLOCK = 256
MOBA_TOPK = 3
Q_BLOCK = 128
ROPE_THETA = 500000.0
ROPE_DIM = HEAD_DIM // 4
N_BRANCH = 3
D_FF = -(-(8 * D_MODEL) // (3 * 256)) * 256
LN_EPS = 1e-5
DN_ALPHA = (2 * DEPTH) ** 0.25
DN_BETA = (8 * DEPTH) ** -0.25
IN_SIZES = (FOX_HEADS * HEAD_DIM, FOX_HEADS * HEAD_DIM, FOX_HEADS * HEAD_DIM, FOX_HEADS,
            DIL_Q_HEADS * HEAD_DIM, DIL_KV_HEADS * HEAD_DIM, DIL_KV_HEADS * HEAD_DIM,
            MOBA_HEADS * HEAD_DIM, MOBA_HEADS * HEAD_DIM, MOBA_HEADS * HEAD_DIM,
            N_BRANCH * D_MODEL)
D_IN = sum(IN_SIZES)

kernel_name = 'hybrid_fox_dilated_moba_deepnorm'

def _layer_norm(x, g, b):
    xf = x.astype(jnp.float32)
    mu = jnp.mean(xf, axis=-1, keepdims=True)
    var = jnp.mean(jnp.square(xf - mu), axis=-1, keepdims=True)
    y = (xf - mu) * lax.rsqrt(var + LN_EPS)
    return (y * g + b).astype(x.dtype)

def _heads(t, n):
    b, s, _ = t.shape
    return t.reshape(b, s, n, HEAD_DIM).transpose(0, 2, 1, 3)

def _merge_heads(t):
    b, h, s, d = t.shape
    return t.transpose(0, 2, 1, 3).reshape(b, s, h * d)

def _rope(t, pos):
    half = ROPE_DIM // 2
    inv_freq = jnp.power(ROPE_THETA, -jnp.arange(half, dtype=jnp.float32) * 2.0 / ROPE_DIM)
    ang = pos.astype(jnp.float32)[:, None] * inv_freq[None, :]
    cos, sin = jnp.cos(ang), jnp.sin(ang)
    t1 = t[..., :half].astype(jnp.float32)
    t2 = t[..., half:ROPE_DIM].astype(jnp.float32)
    rot = jnp.concatenate([t1 * cos - t2 * sin, t2 * cos + t1 * sin], axis=-1).astype(t.dtype)
    return jnp.concatenate([rot, t[..., ROPE_DIM:]], axis=-1)

def _fox_attention(q, k, v, f_logit):
    b, h, s, d = q.shape
    scale = d ** -0.5
    logf = jax.nn.log_sigmoid(f_logit.astype(jnp.float32)).transpose(0, 2, 1)
    c = jnp.cumsum(logf, axis=-1)
    nq = s // Q_BLOCK
    qb = q.reshape(b, h, nq, Q_BLOCK, d).transpose(2, 0, 1, 3, 4)
    cb = c.reshape(b, h, nq, Q_BLOCK).transpose(2, 0, 1, 3)
    kpos = jnp.arange(s)

    def block(args):
        i, qi, ci = args
        logits = jnp.einsum('bhqd,bhkd->bhqk', qi, k, preferred_element_type=jnp.float32) * scale
        logits = logits + ci[..., None] - c[:, :, None, :]
        qpos = i * Q_BLOCK + jnp.arange(Q_BLOCK)
        logits = jnp.where(kpos[None, :] <= qpos[:, None], logits, -jnp.inf)
        p = jax.nn.softmax(logits, axis=-1)
        return jnp.einsum('bhqk,bhkd->bhqd', p.astype(v.dtype), v, preferred_element_type=jnp.float32)

    o = lax.map(block, (jnp.arange(nq), qb, cb))
    return o.transpose(1, 2, 0, 3, 4).reshape(b, h, s, d)

def _dilated_group(q, k, v, window, dil):
    b, h, s, d = q.shape
    scale = d ** -0.5
    span = window // dil
    n_prev = -(-span // Q_BLOCK)
    length = -(-s // (dil * Q_BLOCK)) * Q_BLOCK
    pad = length * dil - s
    nb = length // Q_BLOCK

    def strided(t):
        t = jnp.pad(t, ((0, 0), (0, 0), (0, pad), (0, 0)))
        t = t.reshape(b, h, length, dil, d).transpose(0, 1, 3, 2, 4)
        return t.reshape(b, h, dil, nb, Q_BLOCK, d)

    def band(t):
        tp = jnp.pad(t, ((0, 0), (0, 0), (0, 0), (n_prev, 0), (0, 0), (0, 0)))
        return jnp.concatenate([tp[:, :, :, j:j + nb] for j in range(n_prev + 1)], axis=4)

    qs = strided(q)
    kb, vb = band(strided(k)), band(strided(v))
    logits = jnp.einsum('bhrnqd,bhrnkd->bhrnqk', qs, kb, preferred_element_type=jnp.float32) * scale
    qi = jnp.arange(Q_BLOCK)[:, None] + n_prev * Q_BLOCK
    ki = jnp.arange((n_prev + 1) * Q_BLOCK)[None, :]
    dist = qi - ki
    abs_k = jnp.arange(nb)[:, None, None] * Q_BLOCK - n_prev * Q_BLOCK + ki[None]
    mask = (dist >= 0)[None] & (dist <= span)[None] & (abs_k >= 0)
    logits = jnp.where(mask, logits, -jnp.inf)
    m = jnp.max(logits, axis=-1, keepdims=True)
    p = jnp.exp(logits - m)
    den = jnp.sum(p, axis=-1, keepdims=True)
    o = jnp.einsum('bhrnqk,bhrnkd->bhrnqd', p.astype(v.dtype), vb, preferred_element_type=jnp.float32) / den
    lse = m[..., 0] + jnp.log(den[..., 0])
    o = o.reshape(b, h, dil, length, d).transpose(0, 1, 3, 2, 4).reshape(b, h, length * dil, d)[:, :, :s]
    lse = lse.reshape(b, h, dil, length).transpose(0, 1, 3, 2).reshape(b, h, length * dil)[:, :, :s]
    return o, lse

def _dilated_attention(q, k, v):
    outs, lses = [], []
    for g, (window, dil) in enumerate(DIL_PATTERNS):
        o, l = _dilated_group(q[:, g * DIL_KV_HEADS:(g + 1) * DIL_KV_HEADS], k, v, window, dil)
        outs.append(o)
        lses.append(l)
    w = jax.nn.softmax(jnp.stack(lses, axis=0), axis=0)
    return jnp.sum(w[..., None] * jnp.stack(outs, axis=0), axis=0)

def _moba_attention(q, k, v):
    b, h, s, d = q.shape
    scale = d ** -0.5
    nkb = -(-s // MOBA_BLOCK)
    sp = nkb * MOBA_BLOCK
    kp = jnp.pad(k, ((0, 0), (0, 0), (0, sp - s), (0, 0)))
    vp = jnp.pad(v, ((0, 0), (0, 0), (0, sp - s), (0, 0)))
    kb = kp.reshape(b, h, nkb, MOBA_BLOCK, d)
    vb = vp.reshape(b, h, nkb, MOBA_BLOCK, d)
    kmean = jnp.mean(kb.astype(jnp.float32), axis=3)
    topk = min(MOBA_TOPK, nkb)
    nq = s // Q_BLOCK
    qb = q.reshape(b, h, nq, Q_BLOCK, d).transpose(2, 0, 1, 3, 4)
    bi = jnp.arange(b)[:, None, None, None]
    hi = jnp.arange(h)[None, :, None, None]

    def block(args):
        i, qi = args
        qpos = i * Q_BLOCK + jnp.arange(Q_BLOCK)
        own_blk = (i * Q_BLOCK) // MOBA_BLOCK
        gate = jnp.einsum('bhqd,bhnd->bhqn', qi.astype(jnp.float32), kmean)
        past = jnp.arange(nkb)[None, :] < (qpos // MOBA_BLOCK)[:, None]
        gate = jnp.where(past, gate, -jnp.inf)
        gval, idx = lax.top_k(gate, topk)
        valid = jnp.isfinite(gval)
        ksel = kb[bi, hi, idx]
        vsel = vb[bi, hi, idx]
        s_sel = jnp.einsum('bhqd,bhqnkd->bhqnk', qi, ksel, preferred_element_type=jnp.float32) * scale
        s_sel = jnp.where(valid[..., None], s_sel, -jnp.inf).reshape(b, h, Q_BLOCK, topk * MOBA_BLOCK)
        kown = lax.dynamic_slice_in_dim(kp, own_blk * MOBA_BLOCK, MOBA_BLOCK, axis=2)
        vown = lax.dynamic_slice_in_dim(vp, own_blk * MOBA_BLOCK, MOBA_BLOCK, axis=2)
        s_own = jnp.einsum('bhqd,bhkd->bhqk', qi, kown, preferred_element_type=jnp.float32) * scale
        kpos_own = own_blk * MOBA_BLOCK + jnp.arange(MOBA_BLOCK)
        s_own = jnp.where(kpos_own[None, :] <= qpos[:, None], s_own, -jnp.inf)
        p = jax.nn.softmax(jnp.concatenate([s_sel, s_own], axis=-1), axis=-1)
        p_sel = p[..., :topk * MOBA_BLOCK].reshape(b, h, Q_BLOCK, topk, MOBA_BLOCK).astype(v.dtype)
        p_own = p[..., topk * MOBA_BLOCK:].astype(v.dtype)
        return (jnp.einsum('bhqnk,bhqnkd->bhqd', p_sel, vsel, preferred_element_type=jnp.float32)
                + jnp.einsum('bhqk,bhkd->bhqd', p_own, vown, preferred_element_type=jnp.float32))

    o = lax.map(block, (jnp.arange(nq), qb))
    return o.transpose(1, 2, 0, 3, 4).reshape(b, h, s, d)

def _mixer(x, w_in, b_f, w_pa, w_pb, w_pc, w_o):
    bsz, s, _ = x.shape
    pos = jnp.arange(s)
    hcat = jnp.einsum('bsd,de->bse', x, w_in)
    offsets = [int(o) for o in np.cumsum(IN_SIZES)[:-1]]
    qa, ka, va, fa, qb, kb, vb, qc, kc, vc, g = jnp.split(hcat, offsets, axis=-1)
    ya = _fox_attention(_heads(qa, FOX_HEADS), _heads(ka, FOX_HEADS), _heads(va, FOX_HEADS), fa + b_f)
    yb = _dilated_attention(_rope(_heads(qb, DIL_Q_HEADS), pos), _rope(_heads(kb, DIL_KV_HEADS), pos),
                            _heads(vb, DIL_KV_HEADS))
    yc = _moba_attention(_rope(_heads(qc, MOBA_HEADS), pos), _rope(_heads(kc, MOBA_HEADS), pos),
                         _heads(vc, MOBA_HEADS))
    gates = jax.nn.sigmoid(g.astype(jnp.float32)).reshape(bsz, s, N_BRANCH, D_MODEL)
    merged = (gates[:, :, 0] * jnp.einsum('bse,ed->bsd', _merge_heads(ya).astype(x.dtype), w_pa)
              + gates[:, :, 1] * jnp.einsum('bse,ed->bsd', _merge_heads(yb).astype(x.dtype), w_pb)
              + gates[:, :, 2] * jnp.einsum('bse,ed->bsd', _merge_heads(yc).astype(x.dtype), w_pc))
    return jnp.einsum('bsd,de->bse', merged.astype(x.dtype), w_o)

def _swiglu(x, w_gate, w_up, w_down):
    hid = jax.nn.silu(jnp.einsum('bsd,df->bsf', x, w_gate)) * jnp.einsum('bsd,df->bsf', x, w_up)
    return jnp.einsum('bsf,fd->bsd', hid, w_down)

def setup_inputs(seed: int = 0) -> dict:
    key = jax.random.key(seed)
    ks = jax.random.split(key, 20)
    f32 = jnp.float32
    in_scales = (1.0, 1.0, DN_BETA, 0.1, 1.0, 1.0, DN_BETA, 1.0, 1.0, DN_BETA, 1.0)
    col_scale = jnp.concatenate([jnp.full((n,), sc, f32) for n, sc in zip(IN_SIZES, in_scales)])
    wa = FOX_HEADS * HEAD_DIM
    wb = DIL_KV_HEADS * HEAD_DIM
    wc = MOBA_HEADS * HEAD_DIM
    nrm = lambda k, shp: jax.random.normal(k, shp, f32)
    return {
        'x': nrm(ks[0], (BATCH, SEQ, D_MODEL)),
        'ln_in_g': 1.0 + 0.02 * nrm(ks[1], (D_MODEL,)),
        'ln_in_b': 0.02 * nrm(ks[2], (D_MODEL,)),
        'w_in': nrm(ks[3], (DEPTH, D_MODEL, D_IN)) * D_MODEL ** -0.5 * col_scale,
        'b_f': jax.random.uniform(ks[4], (DEPTH, FOX_HEADS), f32, 2.0, 6.0),
        'w_pa': nrm(ks[5], (DEPTH, wa, D_MODEL)) * wa ** -0.5,
        'w_pb': nrm(ks[6], (DEPTH, wb, D_MODEL)) * wb ** -0.5,
        'w_pc': nrm(ks[7], (DEPTH, wc, D_MODEL)) * wc ** -0.5,
        'w_o': nrm(ks[8], (DEPTH, D_MODEL, D_MODEL)) * D_MODEL ** -0.5 * DN_BETA,
        'ln1_g': 1.0 + 0.02 * nrm(ks[9], (DEPTH, D_MODEL)),
        'ln1_b': 0.02 * nrm(ks[10], (DEPTH, D_MODEL)),
        'w_gate': nrm(ks[11], (DEPTH, D_MODEL, D_FF)) * D_MODEL ** -0.5,
        'w_up': nrm(ks[12], (DEPTH, D_MODEL, D_FF)) * D_MODEL ** -0.5,
        'w_down': nrm(ks[13], (DEPTH, D_FF, D_MODEL)) * D_FF ** -0.5 * DN_BETA,
        'ln2_g': 1.0 + 0.02 * nrm(ks[14], (DEPTH, D_MODEL)),
        'ln2_b': 0.02 * nrm(ks[15], (DEPTH, D_MODEL)),
    }

def reference(x, ln_in_g, ln_in_b, w_in, b_f, w_pa, w_pb, w_pc, w_o, ln1_g, ln1_b,
              w_gate, w_up, w_down, ln2_g, ln2_b):
    x = _layer_norm(x, ln_in_g, ln_in_b)
    for l in range(DEPTH):
        mix = _mixer(x, w_in[l], b_f[l], w_pa[l], w_pb[l], w_pc[l], w_o[l])
        x = _layer_norm(DN_ALPHA * x + mix, ln1_g[l], ln1_b[l])
        ffn = _swiglu(x, w_gate[l], w_up[l], w_down[l])
        x = _layer_norm(DN_ALPHA * x + ffn, ln2_g[l], ln2_b[l])
    return x


_drawn_inputs = setup_inputs


def setup_inputs(seed=0):
    import zlib

    import numpy as np

    out = dict(_drawn_inputs(seed))
    spreads = {}
    factors = {'b_f': 32.824}
    for name, (base, spread) in spreads.items():
        noise = np.random.default_rng([zlib.crc32(name.encode()), seed]).standard_normal(out[name].shape)
        drawn = base * np.exp(spread * noise) if base else spread * noise
        out[name] = __import__('jax').numpy.asarray(drawn.astype(out[name].dtype))
    for name, factor in factors.items():
        out[name] = (out[name] * factor).astype(out[name].dtype)
    return out
```

```python
import math
from contextlib import ExitStack

import concourse.bass as bass
from concourse import mybir

F32 = mybir.dt.float32
F32R = mybir.dt.float32r
I32 = mybir.dt.int32
ALU = mybir.AluOpType
ACT = mybir.ActivationFunctionType

P = 128
D_MODEL, SEQ, DEPTH = 1024, 256, 2
HEAD_DIM, ROPE_HALF = 64, 8
ROPE_THETA = 500000.0
FOX_HEADS, DIL_KV_HEADS, MOBA_HEADS = 6, 4, 6
DIL_PATTERNS = ((128, 1), (512, 4), (2048, 16))
GROUPS = len(DIL_PATTERNS)
D_FF = 2816
LN_EPS = 1e-5
ALPHA = (2 * DEPTH) ** 0.25
SCALE = HEAD_DIM ** -0.5
TT = SEQ // P
KT = D_MODEL // P
NW = 512
D_IN = 6662
GATE0 = D_IN - 3 * D_MODEL
BIG = 1e30
TOP = 3e38

QKV = [
    (0, 512, [("qk", 0, 0, 512)]),
    (512, 512, [("qk", 0, 4, 256), ("v", 0, 0, 256)]),
    (1024, 134, [("v", 0, 256, 128), ("f", 0, 0, FOX_HEADS)]),
    (1158, 512, [("qk", 1, 0, 512)]),
    (1670, 512, [("qk", 1, 4, 512)]),
    (2182, 512, [("v", 1, 0, 256), ("qk", 2, 0, 256)]),
    (2694, 512, [("qk", 2, 2, 512)]),
    (3206, 384, [("v", 2, 0, 384)]),
]
BRANCH_KT = [3, 2, 3]
BRANCH_HEADS = [FOX_HEADS, DIL_KV_HEADS, MOBA_HEADS]
K_PAIR = [3, 6, 3]
HI_SLOTS, RAW_SLOTS = 5, 3
STAGES, PSLOTS = 2, 3
FFN_CHUNKS = D_FF // 256


def layer_pieces(layer, w):
    def rows(m, k0, nk, c0, width):
        return m[layer, k0 * P:(k0 + nk) * P, c0:c0 + width].rearrange("(k p) n -> p k n", p=P)

    out = {}
    order = []

    def piece(name, transfers, nk, cols):
        out[name] = (transfers, nk, cols)
        order.append(name)

    for c, (c0, width, _) in enumerate(QKV):
        for half in range(2):
            piece(("qkv", c, half), [(rows(w["w_in"], 4 * half, 4, c0, width), 0, width)], 4, width)
    for b, name in enumerate(("w_pa", "w_pb", "w_pc")):
        for n in range(2):
            for half in range(2):
                c0 = GATE0 + b * D_MODEL + n * NW
                piece(("gate", b, n, half), [(rows(w["w_in"], 4 * half, 4, c0, NW), 0, NW)], 4, NW)
        for n in range(2):
            piece(("proj", b, n), [(rows(w[name], 0, BRANCH_KT[b], n * NW, NW), 0, NW)], BRANCH_KT[b], NW)
    for half in range(2):
        for n in range(2):
            piece(("wo", half, n), [(rows(w["w_o"], 4 * half, 4, n * NW, NW), 0, NW)], 4, NW)

    def gate_up(c):
        for half in range(2):
            piece(("gu", c, half), [(rows(w["w_gate"], 4 * half, 4, c * 256, 256), 0, 256),
                                    (rows(w["w_up"], 4 * half, 4, c * 256, 256), 256, 256)], 4, NW)

    def down(c):
        piece(("down", c), [(rows(w["w_down"], 2 * c, 2, 0, D_MODEL), 0, D_MODEL)], 2, D_MODEL)

    gate_up(0)
    gate_up(1)
    down(0)
    for c in range(2, FFN_CHUNKS):
        gate_up(c)
        down(c - 1)
    down(FFN_CHUNKS - 1)
    return order, out


class Counts:

    def __init__(self):
        self.n = {}

    def next(self, key):
        self.n[key] = self.n.get(key, 0) + 1
        return self.n[key]


def write_plan(orders, base):
    plan = []
    count = Counts()
    aux = [0]
    gu_use = [0]

    def bank(b):
        return b, count.next(("bank", b))

    def aux_bank():
        aux[0] += 1
        return bank(6 + aux[0] % 2)

    def turn(src, buf, k0, nk, t, dst, dst_k0, ready):
        use = aux_bank()
        plan.append(("turn", src, buf, k0, nk, t, dst, dst_k0, use, ready, count.next("turn")))
        return use

    total = sum(len(o) for o in orders)
    split_next = [0]

    def split():
        i = split_next[0]
        if i < total:
            plan.append(("split", i, release.get(i - HI_SLOTS)))
            split_next[0] += 1

    release = {}

    def mm(i, t, lhs, outs, frees, lhs_ready, full=()):
        plan.append(("mm", i, t, lhs, outs, frees and not full, lhs_ready, full))
        if frees:
            release[i] = ("filled", full[-1]) if full else ("used", count.next("used"))
            split()

    norm = [0]

    def layer_norm(t, src, alpha):
        norm[0] += 1
        plan.append(("norm", t, src, norm[0]))
        return norm[0]

    for _ in range(HI_SLOTS):
        split()
    turned = {}
    for t in range(TT):
        r = layer_norm(t, None, None)
        for j in range(2):
            turned[t] = turn("x", 0, 4 * j, 4, t, "act", 4 * j, ("x", r))

    staged = [0]
    events = []
    for layer, order in enumerate(orders):
        at = {name: base[layer] + n for n, name in enumerate(order)}
        g0 = 3 * layer

        units = [(b, h, t) for b in range(3) for h in range(BRANCH_HEADS[b]) for t in range(TT)]
        stage_of = {}
        tick_at = [0]

        def tick():
            k = tick_at[0]
            tick_at[0] += 1
            if k < len(units):
                b, h, t = units[k]
                if b == 0 and t == 0:
                    plan.append(("decay", layer, h, aux_bank()))
                width = (t + 1) * P
                if b == 1:
                    s = [bank(4)] + ([bank(5)] if t else [])
                else:
                    s = [bank(4 + k % 2)]
                u = layer * len(units) + k
                stage_of[k] = dict(b=b, h=h, t=t, s=s, u=u, w=width, sum_n=count.next("sum") if b == 1 else 0)
                stage_of[k]["qk"] = qk_last[b]
                plan.append(("scores", stage_of[k], g0 + b))
            if 0 <= k - 2 < len(units):
                d = stage_of[k - 2]
                d["pt"] = aux_bank()
                d["last"] = k - 2 == len(units) - 1
                plan.append(("turn_p", d))
            if 0 <= k - 3 < len(units):
                d = stage_of[k - 3]
                d["o"] = aux_bank()
                plan.append(("values", d, g0 + d["b"]))
                last_y[d["b"]] = d["o"]
                if d["h"] == BRANCH_HEADS[d["b"]] - 1 and d["t"] == TT - 1:
                    pend_y.append(d["b"])

        pend_y = []
        last_y = {}
        qk_last = {}
        y_turned = {}
        later = []

        def flush():
            todo, later[:] = list(later), []
            for f in todo:
                f()
            for b in list(pend_y):
                pend_y.remove(b)

                def turn_y(b=b):
                    for t in range(TT):
                        y_turned[b] = turn("y", 0, 0, BRANCH_KT[b], t, "y%d" % ((g0 + b) % 2), 0,
                                           ("bank", last_y[b]))
                turn_y()

        def qkv_done(c, t, use):
            segs = []
            col = 0
            for kind, b, first, width in QKV[c][2]:
                segs.append((kind, b, first, col, width))
                col += width
            ev = None
            for kind, b, first, col, width in segs:
                if kind == "qk":
                    staged[0] += 1
                    ev = dict(e=staged[0], b=b, pair=first, np=width // P, t=t, rope=b > 0, g=g0 + b, col=col)
            plan.append(("spread", layer, c, t, use, segs, ev, g0))
            if ev is not None:
                ev["rope_n"] = count.next("rope") if ev["rope"] else 0
                ev["use"] = use
                events.append(ev)
                ev["prev"] = events[-1 - STAGES] if len(events) > STAGES else None

                def turn_qk(ev=ev):
                    ev["bank"] = aux_bank()
                    qk_last[ev["b"]] = ev["bank"]
                    plan.append(("turn_qk", ev))
                later.append(turn_qk)

        def qkv(c, t, halves, use, frees, tick_too):
            for half in halves:
                mm(at[("qkv", c, half)], t, ("act", 4 * half), [(use, 0, QKV[c][1], half == 0, half == 1)],
                   frees, turned[t], (use,) if half else ())
                if tick_too and not (half == 1):
                    flush()
                    tick()
            if halves[-1] == 1:
                flush()
                qkv_done(c, t, use)
                if tick_too:
                    tick()

        for t in range(TT):
            for c in range(2):
                qkv(c, t, (0, 1), bank(2 * c + t), t == TT - 1, False)
        for c in range(2, len(QKV)):
            use = [bank(2 * (c % 2) + t) for t in range(TT)]
            for half in range(2):
                for t in range(TT):
                    qkv(c, t, (half,), use[t], t == TT - 1, c > 2)
            if c == 2:
                plan.append(("forget", layer, aux_bank(), use[TT - 1]))

        merged_done = {}

        def gates(b):
            for n in range(2):
                use = [bank(2 * n + t) for t in range(TT)]
                for half in range(2):
                    for t in range(TT):
                        mm(at[("gate", b, n, half)], t, ("act", 4 * half), [(use[t], 0, NW, half == 0, half == 1)],
                           t == TT - 1, turned[t], (use[t],) if half else ())
                        flush()
                        if half:
                            plan.append(("gate", n, t, use[t], merged_done.get((n, t)) if b == 2 else None))
                        if tick_at[0] < len(units) + 3:
                            tick()

        def proj(b):
            for n in range(2):
                for t in range(TT):
                    use = bank(2 * n + t)
                    mm(at[("proj", b, n)], t, ("y%d" % ((g0 + b) % 2), 0), [(use, 0, NW, True, True)],
                       t == TT - 1, y_turned[b], (use,))
                    flush()
                    plan.append(("merge", b, n, t, use))
                    if b > 0:
                        merged_done[n, t] = count.next("merge")
                    if tick_at[0] < len(units) + 3:
                        tick()

        for b in range(3):
            gates(b)
            proj(b)

        def turn_merged(n, t):
            turned["m", n, t] = turn("merged", 0, 4 * n, 4, t, "act", 4 * n, ("merge", merged_done[n, t]))

        for n in range(2):
            turn_merged(0, n)
        norm_r = {}
        wo_use = {}
        for t in range(TT):
            wo_use[t] = [bank(2 * n + t) for n in range(2)]
            for half in range(2):
                for n in range(2):
                    mm(at[("wo", half, n)], t, ("act", 4 * half), [(wo_use[t][n], 0, NW, half == 0, half == 1)],
                       t == TT - 1, turned["m", half, t], (wo_use[t][n],) if half else ())
                    if half == 0 and n == 0 and t == 0:
                        turn_merged(1, 0)
                        turn_merged(1, 1)
            norm_r[t] = layer_norm(t, wo_use[t], ALPHA)

        def turn_x(t):
            for j in range(2):
                turned[t] = turn("x", 0, 4 * j, 4, t, "act", 4 * j, ("x", norm_r[t]))

        hid = {}

        def gu_bank():
            gu_use[0] += 1
            return bank(4 + gu_use[0] % 2)

        def gate_up(c, t, half, use, frees):
            mm(at[("gu", c, half)], t, ("act", 4 * half), [(use, 0, NW, half == 0, half == 1)],
               frees, turned[t], (use,) if half else ())
            if half:
                hid[c, t] = use
                plan.append(("hidden", c, t, use, count.next("hid")))

        def turn_hid(c, t):
            turned["h", c, t] = turn("hid", c % 2, 0, 2, t, "y%d" % (c % 2), 0, ("bank", hid[c, t]))

        down_use = {t: None for t in range(TT)}

        def down(c, t, frees):
            if c == 0:
                down_use[t] = [bank(2 * n + t) for n in range(2)]
            last = c == FFN_CHUNKS - 1
            mm(at[("down", c)], t, ("y%d" % (c % 2), 0),
               [(down_use[t][n], n * NW, NW, c == 0, last) for n in range(2)],
               frees, turned["h", c, t], tuple(down_use[t]) if last else ())

        for t in range(TT):
            turn_x(t)
            for c in range(2):
                use = gu_bank()
                for half in range(2):
                    gate_up(c, t, half, use, t == TT - 1)
                if t or c:
                    turn_hid(*((c - 1, t) if c else (1, t - 1)))
        down(0, 0, False)
        down(0, 1, True)
        turn_hid(1, 1)
        for c in range(2, FFN_CHUNKS):
            use = [gu_bank() for _ in range(TT)]
            for t in range(TT):
                gate_up(c, t, 0, use[t], t == TT - 1)
            if c > 2:
                for t in range(TT):
                    turn_hid(c - 1, t)
            for t in range(TT):
                gate_up(c, t, 1, use[t], t == TT - 1)
            if c < FFN_CHUNKS - 1:
                for t in range(TT):
                    down(c - 1, t, t == TT - 1)
        last = FFN_CHUNKS - 1
        for t in range(TT):
            down(last - 1, t, t == TT - 1)
            turn_hid(last, t)
            down(last, t, t == TT - 1)
            norm_r[t] = layer_norm(t, down_use[t], ALPHA)
        if layer < DEPTH - 1:
            for t in range(TT):
                turn_x(t)
    return plan


TABLE_COLS = P + SEQ + SEQ + GROUPS * SEQ + 2 * TT * ROPE_HALF


def norm_params(d, j):
    if j == 0:
        return d["ln_in_g"], d["ln_in_b"]
    layer, second = (j - 1) // 2, (j - 1) % 2
    name = "ln2" if second else "ln1"
    return d[name + "_g"][layer], d[name + "_b"][layer]


def trunk(nc, d):
    orders, pieces, base = [], [], []
    for layer in range(DEPTH):
        order, table = layer_pieces(layer, d)
        base.append(len(pieces))
        orders.append(order)
        pieces += [table[name] for name in order]
    PLAN = write_plan(orders, base)

    with ExitStack() as ctx:
        def sb(name, shape, dtype=F32):
            return ctx.enter_context(nc.sbuf_tensor(name, shape, dtype))

        def sem(name):
            return ctx.enter_context(nc.semaphore(name))

        bank = [ctx.enter_context(nc.psum_tensor(f"bank{b}", [P, 512], F32)) for b in range(8)]
        raw = [sb(f"raw{s}", [P, 2048]) for s in range(RAW_SLOTS)]
        w_hi = [sb(f"w_hi{s}", [P, 2048], F32R) for s in range(HI_SLOTS)]
        w_lo = [sb(f"w_lo{s}", [P, 2048], F32R) for s in range(HI_SLOTS)]
        x = [sb(f"x{t}", [P, D_MODEL]) for t in range(TT)]
        hi = {n: sb(n + "_hi", [P, k, SEQ], F32R) for n, k in
              (("act", KT), ("y0", 3), ("y1", 3))}
        lo = {n: sb(n + "_lo", [P, k, SEQ], F32R) for n, k in
              (("act", KT), ("y0", 3), ("y1", 3))}
        values = [sb(f"values{s}", [P, TT, 384]) for s in range(2)]
        qk_t = [sb(f"qk_t{s}", [P, 8, SEQ]) for s in range(2)]
        stage = [sb(f"stage{s}", [P, 512]) for s in range(STAGES)]
        shared = sb("shared", [P, PSLOTS * GROUPS * SEQ])
        prob = [shared[:, s * GROUPS * SEQ:(s + 1) * GROUPS * SEQ] for s in range(PSLOTS)]
        gain_bias = shared[:, 0:2 * D_MODEL].rearrange("p (a n) -> p a n", a=2)
        prob_t = [sb(f"prob_t{s}", [P, SEQ]) for s in range(2)]
        y = sb("y", [P, TT, 384])
        act_fn = [sb(f"act_fn{s}", [P, 512]) for s in range(4)]
        merged = [sb(f"merged{t}", [P, D_MODEL]) for t in range(TT)]
        tables = sb("tables", [P, TABLE_COLS])
        decay = [sb(f"decay{s}", [P, 3 * P]) for s in range(2)]
        neg_max = sb("neg_max", [P, 4])
        denom = sb("denom", [P, 4])
        rdenom = sb("rdenom", [P, 4])
        f_bias = sb("f_bias", [P, DEPTH, FOX_HEADS])
        f_in = sb("f_in", [P, TT, FOX_HEADS])
        f_neg_abs = sb("f_neg_abs", [P, TT, FOX_HEADS])
        f_exp = sb("f_exp", [P, TT, FOX_HEADS])
        neg_logf = sb("neg_logf", [P, TT, FOX_HEADS])
        neg_cum = sb("neg_cum", [P, TT, FOX_HEADS])
        rope_cos = sb("rope_cos", [P, 8, 2, ROPE_HALF])
        rope_sin = sb("rope_sin", [P, 8, 2, ROPE_HALF])
        stats = sb("stats", [P, 2, 6])
        mean_var = sb("mean_var", [P, 2])
        var_eps = sb("var_eps", [P, 1])
        rstd = sb("rstd", [P, 1])
        newton = sb("newton", [P, 1])

        col = 0

        def table(width):
            nonlocal col
            col += width
            return tables[:, col - width:col]

        ident = table(P)
        upper = table(SEQ)
        causal = table(SEQ)
        dil_mask = table(GROUPS * SEQ).rearrange("p (g k) -> p g k", g=GROUPS)
        cos = table(TT * ROPE_HALF).rearrange("p (t i) -> p t i", t=TT)
        sin = table(TT * ROPE_HALF).rearrange("p (t i) -> p t i", t=TT)

        raw_full = [sem(f"raw_full{s}") for s in range(RAW_SLOTS)]
        filled = [sem(f"filled{b}") for b in range(8)]
        drained = [sem(f"drained{b}") for b in range(8)]
        hi_done = sem("hi_done")
        lo_done = sem("lo_done")
        piece_used = sem("piece_used")
        turn_hi = sem("turn_hi")
        roped = sem("roped")
        exp_done = sem("exp_done")
        summed = sem("summed")
        silu_done = sem("silu_done")
        merge_done = sem("merge_done")
        x_ready = sem("x_ready")
        x_loaded = sem("x_loaded")
        gb_loaded = sem("gb_loaded")
        tables_loaded = sem("tables_loaded")
        neg_abs_ready = sem("neg_abs_ready")
        log_ready = sem("log_ready")
        logf_ready = sem("logf_ready")
        act_own = sem("act_own")
        dve_own = sem("dve_own")
        pool_own = sem("pool_own")
        out_done = sem("out_done")

        raw_count, so_far = [], [0] * RAW_SLOTS
        for i, (transfers, _, _) in enumerate(pieces):
            so_far[i % RAW_SLOTS] += 16 * len(transfers)
            raw_count.append(so_far[i % RAW_SLOTS])

        def weights(ring, i, n_rows):
            _, nk, cols = pieces[i]
            return ring[i % n_rows][:, 0:nk * cols]

        def source(src, buf, k, t):
            if src == "x":
                return x[t][:, k * P:(k + 1) * P]
            if src == "y":
                return y[:, t, k * P:(k + 1) * P]
            if src == "merged":
                return merged[t][:, k * P:(k + 1) * P]
            return act_fn[2 * buf + t][:, 256 + k * P:256 + (k + 1) * P]

        def group_view(ap, groups, width):
            return ap[:, 0:groups * width].rearrange("p (g k) -> p g k", g=groups)

        block = ctx.enter_context(nc.Block())

        @block.sync
        def _(sp):
            def load_gain_bias(j):
                g, b = norm_params(d, j)
                if j % 2:
                    b_pt, n_pt = last_probs
                    sp.wait_ge(filled[b_pt], n_pt)
                elif j:
                    sp.wait_ge(x_ready, TT * j)
                sp.dma_start(gain_bias[:, 0, :], g.partition_broadcast(P)).then_inc(gb_loaded, 16)
                sp.dma_start(gain_bias[:, 1, :], b.partition_broadcast(P)).then_inc(gb_loaded, 16)

            last_probs = None
            for t in range(TT):
                sp.dma_start(x[t][:, :], d["x"][t * P:(t + 1) * P, :]).then_inc(x_loaded, 16)
            load_gain_bias(0)
            sp.dma_start(tables[:, :], d["tables"]).then_inc(tables_loaded, 16)
            sp.dma_start(f_bias[:, :, :].rearrange("p l h -> p (l h)"),
                         d["b_f"].rearrange("l h -> (l h)").partition_broadcast(P)).then_inc(tables_loaded, 16)
            norms, put_off = 0, None
            for step in PLAN:
                if step[0] == "split":
                    i = step[1]
                    transfers, nk, cols = pieces[i]
                    if i >= RAW_SLOTS:
                        sp.wait_ge(lo_done, i - RAW_SLOTS + 1)
                    dst = weights(raw, i, RAW_SLOTS).rearrange("p (k n) -> p k n", k=nk)
                    for src, c0, width in transfers:
                        sp.dma_start(dst[:, :, c0:c0 + width], src).then_inc(raw_full[i % RAW_SLOTS], 16)
                    if put_off is not None:
                        put_off -= 1
                        if put_off == 0:
                            load_gain_bias(norms // TT)
                            put_off = None
                elif step[0] == "norm":
                    norms += 1
                    if norms % TT == 0 and (norms // TT) % 2 == 0 and norms // TT <= 2 * DEPTH:
                        put_off = RAW_SLOTS
                elif step[0] == "turn_p" and step[1]["last"]:
                    last_probs = step[1]["pt"]
                    put_off = RAW_SLOTS
            for t in range(TT):
                sp.wait_ge(x_ready, TT * 2 * DEPTH + t + 1)
                sp.dma_start(d["out"][t * P:(t + 1) * P, :], x[t][:, :]).then_inc(out_done, 16)
            sp.wait_ge(out_done, 16 * TT)

        @block.gpsimd
        def _(pool):
            own = 0

            def link(ins):
                nonlocal own
                own += 1
                ins.then_inc(pool_own, 1)
                pool.wait_ge(pool_own, own)

            pool.wait_ge(tables_loaded, 32)
            for step in PLAN:
                if step[0] == "spread" and step[6] is not None and step[6]["rope"]:
                    ev = step[6]
                    b, n = ev["use"]
                    heads = 2 * ev["np"]
                    t = ev["t"]
                    v = stage[ev["e"] % STAGES][:, 0:heads * HEAD_DIM].rearrange(
                        "p (h d) -> p h d", d=HEAD_DIM)[:, :, 0:2 * ROPE_HALF].rearrange(
                        "p h (a i) -> p h a i", a=2)
                    c4 = cos[:, t, :].unsqueeze(1).unsqueeze(1).broadcast_to([P, heads, 2, ROPE_HALF])
                    s4 = sin[:, t, :].unsqueeze(1).unsqueeze(1).broadcast_to([P, heads, 2, ROPE_HALF])
                    rc, rs = rope_cos[:, 0:heads], rope_sin[:, 0:heads]
                    pool.wait_ge(drained[b], n)
                    link(pool.tensor_tensor(rc, v, c4, ALU.mult))
                    link(pool.tensor_tensor(rs, v, s4, ALU.mult))
                    link(pool.tensor_tensor(v[:, :, 0, :], rc[:, :, 0, :], rs[:, :, 1, :], ALU.subtract))
                    pool.tensor_tensor(v[:, :, 1, :], rc[:, :, 1, :], rs[:, :, 0, :], ALU.add).then_inc(roped, 1)
                    pool.wait_ge(roped, ev["rope_n"])
                elif step[0] == "scores" and step[1]["b"] == 1:
                    u = step[1]
                    w = u["w"]
                    pr = group_view(prob[u["u"] % PSLOTS], GROUPS, w)
                    pool.wait_ge(exp_done, u["u"] + 1)
                    link(pool.tensor_tensor(pr[:, 0, :], pr[:, 0, :], pr[:, 1, :], ALU.add))
                    pool.tensor_tensor(pr[:, 0, :], pr[:, 0, :], pr[:, 2, :], ALU.add).then_inc(summed, 1)

        @block.scalar
        def _(act):
            own = 0

            def link(ins):
                nonlocal own
                own += 1
                ins.then_inc(act_own, 1)
                act.wait_ge(act_own, own)

            for step in PLAN:
                kind = step[0]
                if kind == "split":
                    i = step[1]
                    act.wait_ge(raw_full[i % RAW_SLOTS], raw_count[i])
                    if i >= HI_SLOTS:
                        how, r = step[2]
                        if how == "filled":
                            act.wait_ge(filled[r[0]], r[1])
                        else:
                            act.wait_ge(piece_used, r)
                    act.copy(weights(w_hi, i, HI_SLOTS), weights(raw, i, RAW_SLOTS)).then_inc(hi_done, 1)
                elif kind == "turn":
                    _, src, buf, k0, nk, t, dst, dk, (b, n), _, idx = step
                    act.wait_ge(filled[b], n)
                    act.copy(hi[dst][:, dk:dk + nk, t * P:(t + 1) * P],
                             group_view(bank[b], nk, P)).then_inc(turn_hi, 1)
                elif kind == "spread":
                    _, layer, c, t, (b, n), segs, ev, g0 = step
                    act.wait_ge(filled[b], n)
                    for s, (what, br, first, col0, width) in enumerate(segs):
                        src = bank[b][:, col0:col0 + width]
                        if what == "qk":
                            if ev["prev"] is not None:
                                pb_, pn = ev["prev"]["bank"]
                                act.wait_ge(filled[pb_], pn)
                            out = stage[ev["e"] % STAGES][:, 0:width]
                        elif what == "v":
                            out = values[(g0 + br) % 2][:, t, first:first + width]
                        else:
                            out = f_in[:, t, :]
                        ins = act.copy(out, src)
                    ins.then_inc(drained[b], 1)
                elif kind == "forget":
                    _, layer, _, _ = step
                    act.wait_ge(neg_abs_ready, layer + 1)
                    link(act.activation(f_exp[:, :, :], f_neg_abs[:, :, :], ACT.Exp))
                    act.activation(f_exp[:, :, :], f_exp[:, :, :], ACT.Ln, bias=1.0).then_inc(log_ready, 1)
                elif kind == "scores":
                    u = step[1]
                    b, n = u["s"][-1]
                    slot = u["u"] % 4
                    pr = prob[u["u"] % PSLOTS][:, 0:(GROUPS if u["b"] == 1 else 1) * u["w"]]
                    act.wait_ge(drained[b], n)
                    act.activation(pr, pr, ACT.Exp, bias=neg_max[:, slot:slot + 1], scale=-1.0,
                                   accum_out=denom[:, slot:slot + 1]).then_inc(exp_done, 1)
                elif kind == "turn_p":
                    u = step[1]
                    b, n = u["pt"]
                    act.wait_ge(filled[b], n)
                    act.copy(prob_t[u["u"] % 2][:, 0:u["w"]], bank[b][:, 0:u["w"]]).then_inc(drained[b], 1)
                elif kind == "gate":
                    _, nh, t, (b, n), last_merge = step
                    act.wait_ge(filled[b], n)
                    if last_merge is not None:
                        act.wait_ge(merge_done, last_merge)
                    act.activation(act_fn[2 * nh + t][:, :], bank[b][:, :], ACT.Sigmoid).then_inc(drained[b], 1)
                elif kind == "hidden":
                    _, c, t, (b, n), _ = step
                    act.wait_ge(filled[b], n)
                    act.activation(act_fn[2 * (c % 2) + t][:, 0:256], bank[b][:, 0:256],
                                   ACT.Silu).then_inc(silu_done, 1)

        @block.vector
        def _(dve):
            own = 0

            def link(ins):
                nonlocal own
                own += 1
                ins.then_inc(dve_own, 1)
                dve.wait_ge(dve_own, own)

            dve.wait_ge(tables_loaded, 32)
            for step in PLAN:
                kind = step[0]
                if kind == "split":
                    i = step[1]
                    dve.wait_ge(hi_done, i + 1)
                    dve.tensor_tensor(weights(w_lo, i, HI_SLOTS), weights(raw, i, RAW_SLOTS),
                                      weights(w_hi, i, HI_SLOTS).bitcast(F32), ALU.subtract).then_inc(lo_done, 1)
                elif kind == "turn":
                    _, src, buf, k0, nk, t, dst, dk, (b, n), _, idx = step
                    dve.wait_ge(turn_hi, idx)
                    dve.tensor_tensor(lo[dst][:, dk:dk + nk, t * P:(t + 1) * P], group_view(bank[b], nk, P),
                                      hi[dst][:, dk:dk + nk, t * P:(t + 1) * P].bitcast(F32),
                                      ALU.subtract).then_inc(drained[b], 1)
                elif kind == "turn_qk":
                    ev = step[1]
                    b, n = ev["bank"]
                    dve.wait_ge(filled[b], n)
                    dve.tensor_copy(qk_t[ev["g"] % 2][:, ev["pair"]:ev["pair"] + ev["np"],
                                                      ev["t"] * P:(ev["t"] + 1) * P],
                                    group_view(bank[b], ev["np"], P)).then_inc(drained[b], 1)
                elif kind == "forget":
                    _, layer, (b, n), (fb, fn) = step
                    dve.wait_ge(drained[fb], fn)
                    link(dve.tensor_tensor(f_in[:, :, :], f_in[:, :, :],
                                           f_bias[:, layer, :].unsqueeze(1).broadcast_to([P, TT, FOX_HEADS]),
                                           ALU.add))
                    dve.scalar_tensor_tensor(out=f_neg_abs[:, :, :], in0=f_in[:, :, :], scalar=-1.0, in1=f_in[:, :, :],
                                             op0=ALU.mult, op1=ALU.min).then_inc(neg_abs_ready, 1)
                    dve.wait_ge(log_ready, layer + 1)
                    link(dve.scalar_tensor_tensor(out=neg_logf[:, :, :], in0=f_in[:, :, :], scalar=0.0,
                                                  in1=f_exp[:, :, :], op0=ALU.min, op1=ALU.subtract))
                    dve.tensor_scalar(neg_logf[:, :, :], neg_logf[:, :, :], -1.0 / SCALE, None,
                                      ALU.mult).then_inc(logf_ready, 1)
                    dve.wait_ge(filled[b], n)
                    dve.tensor_copy(neg_cum[:, :, :], group_view(bank[b], TT, FOX_HEADS)).then_inc(drained[b], 1)
                    dve.wait_ge(drained[b], n)
                elif kind == "decay":
                    _, layer, h, (b, n) = step
                    dve.wait_ge(filled[b], n)
                    dk = decay[h % 2]
                    link(dve.scalar_tensor_tensor(out=dk[:, 0:P], in0=bank[b][:, 0:P],
                                                  scalar=neg_cum[:, 0, h:h + 1], in1=causal[:, P:SEQ],
                                                  op0=ALU.subtract, op1=ALU.add))
                    dve.scalar_tensor_tensor(out=dk[:, P:3 * P], in0=bank[b][:, 0:SEQ],
                                             scalar=neg_cum[:, 1, h:h + 1], in1=causal,
                                             op0=ALU.subtract, op1=ALU.add).then_inc(drained[b], 1)
                    dve.wait_ge(drained[b], n)
                elif kind == "scores":
                    u = step[1]
                    t, w, slot = u["t"], u["w"], u["u"] % 4
                    pr = prob[u["u"] % PSLOTS]
                    nm = neg_max[:, slot:slot + 1]
                    k0 = SEQ - w
                    if u["b"] == 1:
                        first = GROUPS if t == 0 else 2
                        b, n = u["s"][0]
                        pv = group_view(pr, GROUPS, w)
                        dve.wait_ge(filled[b], n)
                        dve.tensor_tensor_reduce(pv[:, 0:first, :], group_view(bank[b], first, w),
                                                 dil_mask[:, 0:first, k0:SEQ], -SCALE, TOP, ALU.add, ALU.min,
                                                 nm).then_inc(drained[b], 1)
                        if t:
                            dve.wait_ge(drained[b], n)
                            b, n = u["s"][1]
                            dve.wait_ge(filled[b], n)
                            dve.tensor_tensor_reduce(pv[:, 2, :], bank[b][:, 0:w], dil_mask[:, 2, k0:SEQ],
                                                     -SCALE, nm, ALU.add, ALU.min, nm).then_inc(drained[b], 1)
                    else:
                        b, n = u["s"][0]
                        if u["b"] == 0:
                            mask = decay[u["h"] % 2][:, 0:P] if t == 0 else decay[u["h"] % 2][:, P:3 * P]
                        else:
                            mask = causal[:, k0:SEQ]
                        dve.wait_ge(filled[b], n)
                        dve.tensor_tensor_reduce(pr[:, 0:w], bank[b][:, 0:w], mask, -SCALE, TOP, ALU.add,
                                                 ALU.min, nm).then_inc(drained[b], 1)
                elif kind == "values":
                    u = step[1]
                    b, n = u["o"]
                    slot = u["u"] % 4
                    dve.wait_ge(filled[b], n)
                    link(dve.reciprocal(rdenom[:, slot:slot + 1], denom[:, slot:slot + 1]))
                    dve.tensor_scalar(y[:, u["t"], u["h"] * HEAD_DIM:(u["h"] + 1) * HEAD_DIM],
                                      bank[b][:, 0:HEAD_DIM], rdenom[:, slot:slot + 1], None,
                                      ALU.mult).then_inc(drained[b], 1)
                elif kind == "merge":
                    _, br, nh, t, (b, n) = step
                    dve.wait_ge(filled[b], n)
                    out = merged[t][:, nh * NW:(nh + 1) * NW]
                    sig = act_fn[2 * nh + t][:, :]
                    if br == 0:
                        dve.tensor_tensor(out, sig, bank[b][:, :], ALU.mult).then_inc(drained[b], 1)
                    else:
                        dve.tensor_tensor(sig, sig, bank[b][:, :], ALU.mult).then_inc(drained[b], 1)
                        dve.wait_ge(drained[b], n)
                        dve.tensor_tensor(out, out, sig, ALU.add).then_inc(merge_done, 1)
                elif kind == "hidden":
                    _, c, t, (b, n), idx = step
                    dve.wait_ge(silu_done, idx)
                    a = act_fn[2 * (c % 2) + t]
                    dve.tensor_tensor(a[:, 256:512], a[:, 0:256], bank[b][:, 256:512],
                                      ALU.mult).then_inc(drained[b], 1)
                elif kind == "norm":
                    _, t, src, idx = step
                    xt = x[t]
                    if src is None:
                        dve.wait_ge(x_loaded, 16 * TT)
                    for nh in range(2):
                        xh = xt[:, nh * NW:(nh + 1) * NW]
                        if src is not None:
                            b, n = src[nh]
                            dve.wait_ge(filled[b], n)
                            dve.scalar_tensor_tensor(out=xh, in0=xh, scalar=ALPHA, in1=bank[b][:, :],
                                                     op0=ALU.mult, op1=ALU.add).then_inc(drained[b], 1)
                            dve.wait_ge(drained[b], n)
                        link(dve.bn_stats(stats[:, nh, :], xh))
                    link(dve.bn_aggr(mean_var[:, :], stats[:, :, :]))
                    link(dve.tensor_scalar(var_eps[:, :], mean_var[:, 1:2], LN_EPS, None, ALU.add))
                    link(dve.tensor_scalar(rstd[:, :].bitcast(I32), var_eps[:, :].bitcast(I32), -0.5,
                                           float(0x5F3759DF), ALU.mult, ALU.add))
                    for _ in range(3):
                        link(dve.scalar_tensor_tensor(out=newton[:, :], in0=rstd[:, :], scalar=var_eps[:, 0:1],
                                                      in1=rstd[:, :], op0=ALU.mult, op1=ALU.mult))
                        link(dve.tensor_scalar(newton[:, :], newton[:, :], -0.5, 1.5, ALU.mult, ALU.add))
                        link(dve.tensor_tensor(rstd[:, :], rstd[:, :], newton[:, :], ALU.mult))
                    link(dve.tensor_scalar(xt[:, :], xt[:, :], mean_var[:, 0:1], rstd[:, 0:1],
                                           ALU.subtract, ALU.mult))
                    dve.wait_ge(gb_loaded, 32 * ((idx + 1) // TT))
                    link(dve.tensor_tensor(xt[:, :], xt[:, :], gain_bias[:, 0, :], ALU.mult))
                    dve.tensor_tensor(xt[:, :], xt[:, :], gain_bias[:, 1, :], ALU.add).then_inc(x_ready, 1)
                    dve.wait_ge(x_ready, idx)

        @block.tensor
        def _(pe):
            def take(use):
                b, n = use
                if n > 1:
                    pe.wait_ge(drained[b], n - 1)
                return bank[b], filled[b]

            pe.wait_ge(tables_loaded, 32)
            for step in PLAN:
                kind = step[0]
                if kind == "mm":
                    _, i, t, (lhs, k0), outs, frees, (lb, ln), full = step
                    _, nk, cols = pieces[i]
                    pe.wait_ge(drained[lb], ln)
                    pe.wait_ge(lo_done, i + 1)
                    wh = weights(w_hi, i, HI_SLOTS).rearrange("p (k n) -> p k n", k=nk)
                    wl = weights(w_lo, i, HI_SLOTS).rearrange("p (k n) -> p k n", k=nk)
                    for use, _, _, start, _ in outs:
                        if start:
                            take(use)
                    for o, (use, c0, width, start, stop) in enumerate(outs):
                        for k in range(nk):
                            xh = hi[lhs][:, k0 + k, t * P:(t + 1) * P]
                            xl = lo[lhs][:, k0 + k, t * P:(t + 1) * P]
                            for p, (a, w) in enumerate(((xh, wh), (xh, wl), (xl, wh))):
                                ins = pe.matmul(bank[use[0]][:, 0:width], a, w[:, k, c0:c0 + width],
                                                start=start and k == 0 and p == 0,
                                                stop=stop and k == nk - 1 and p == 2)
                        if use in full:
                            ins.then_inc(filled[use[0]], 1)
                    if frees:
                        ins.then_inc(piece_used, 1)
                elif kind == "turn":
                    _, src, buf, k0, nk, t, dst, dk, use, (what, r), idx = step
                    if what == "bank":
                        pe.wait_ge(drained[r[0]], r[1])
                    else:
                        pe.wait_ge({"x": x_ready, "merge": merge_done}[what], r)
                    out, done = take(use)
                    for k in range(nk):
                        ins = pe.transpose(out[:, k * P:(k + 1) * P], source(src, buf, k0 + k, t), ident)
                    ins.then_inc(done, 1)
                elif kind == "turn_qk":
                    ev = step[1]
                    if ev["rope"]:
                        pe.wait_ge(roped, ev["rope_n"])
                    else:
                        pe.wait_ge(drained[ev["use"][0]], ev["use"][1])
                    out, done = take(ev["bank"])
                    for k in range(ev["np"]):
                        ins = pe.transpose(out[:, k * P:(k + 1) * P],
                                           stage[ev["e"] % STAGES][:, k * P:(k + 1) * P], ident)
                    ins.then_inc(done, 1)
                elif kind == "forget":
                    _, layer, use, _ = step
                    pe.wait_ge(logf_ready, layer + 1)
                    out, done = take(use)
                    pe.matmul(out[:, 0:FOX_HEADS], upper[:, 0:P], neg_logf[:, 0, :], start=True, stop=True)
                    pe.matmul(out[:, FOX_HEADS:2 * FOX_HEADS], upper[:, P:SEQ], neg_logf[:, 0, :],
                              start=True, stop=False)
                    pe.matmul(out[:, FOX_HEADS:2 * FOX_HEADS], upper[:, 0:P], neg_logf[:, 1, :],
                              start=False, stop=True).then_inc(done, 1)
                elif kind == "decay":
                    _, layer, h, use = step
                    out, done = take(use)
                    pe.matmul(out[:, 0:SEQ], neg_logf[:, 0, h:h + 1].broadcast_to([P, P]), upper[:, :],
                              start=True, stop=False)
                    pe.matmul(out[:, P:SEQ], neg_logf[:, 1, h:h + 1].broadcast_to([P, P]), upper[:, 0:P],
                              start=False, stop=True).then_inc(done, 1)
                elif kind == "scores":
                    _, u, g = step
                    br, h, t, w = u["b"], u["h"], u["t"], u["w"]
                    qb, qn = u["qk"]
                    pe.wait_ge(drained[qb], qn)
                    at = (h % 2) * HEAD_DIM
                    keys = qk_t[g % 2][at:at + HEAD_DIM, K_PAIR[br] + h // 2, 0:w]
                    for gi in range(GROUPS if br == 1 else 1):
                        q = h + gi * DIL_KV_HEADS
                        use = u["s"][1] if gi == 2 and t else u["s"][0]
                        if gi == 0 or (gi == 2 and t):
                            take(use)
                            off = 0
                        queries = qk_t[g % 2][at:at + HEAD_DIM, q // 2, t * P:(t + 1) * P]
                        ins = pe.matmul(bank[use[0]][:, off:off + w], queries, keys, start=True, stop=True)
                        off += w
                        if br != 1 or gi == 2 or (gi == 1 and t):
                            ins.then_inc(filled[use[0]], 1)
                elif kind == "turn_p":
                    u = step[1]
                    if u["b"] == 1:
                        pe.wait_ge(summed, u["sum_n"])
                    else:
                        pe.wait_ge(exp_done, u["u"] + 1)
                    out, done = take(u["pt"])
                    for j in range(u["t"] + 1):
                        ins = pe.transpose(out[:, j * P:(j + 1) * P],
                                           prob[u["u"] % PSLOTS][:, j * P:(j + 1) * P], ident)
                    ins.then_inc(done, 1)
                elif kind == "values":
                    _, u, g = step
                    pb_, pn = u["pt"]
                    pe.wait_ge(drained[pb_], pn)
                    out, done = take(u["o"])
                    h = u["h"]
                    for j in range(u["t"] + 1):
                        ins = pe.matmul(out[:, 0:HEAD_DIM], prob_t[u["u"] % 2][:, j * P:(j + 1) * P],
                                        values[g % 2][:, j, h * HEAD_DIM:(h + 1) * HEAD_DIM],
                                        start=j == 0, stop=j == u["t"])
                    ins.then_inc(done, 1)


def constant_tables():
    import numpy as np

    row = np.arange(P)[:, None]
    col = np.arange(SEQ)[None, :]
    f32 = np.float32
    ident = np.eye(P, dtype=f32)
    upper = np.where(row <= col, 1.0, 0.0).astype(f32)
    back = row + P - col
    causal = np.where(back >= 0, 0.0, -BIG).astype(f32)
    dil = [np.where((back >= 0) & (back % dil == 0) & (back // dil <= window // dil), 0.0, -BIG).astype(f32)
           for window, dil in DIL_PATTERNS]
    freq = np.power(f32(ROPE_THETA), -np.arange(ROPE_HALF, dtype=f32) * f32(2.0) / f32(2 * ROPE_HALF)).astype(f32)
    angle = [(np.arange(t * P, (t + 1) * P, dtype=f32)[:, None] * freq[None, :]).astype(f32) for t in range(TT)]
    parts = [ident, upper, causal, *dil, *[np.cos(a) for a in angle], *[np.sin(a) for a in angle]]
    return np.ascontiguousarray(np.concatenate(parts, axis=1).astype(f32))


_INS = ["x", "ln_in_g", "ln_in_b", "w_in", "b_f", "w_pa", "w_pb", "w_pc", "w_o", "ln1_g", "ln1_b",
        "w_gate", "w_up", "w_down", "ln2_g", "ln2_b"]


def kernel(**inputs):
    import numpy as np
    import concourse.bacc as bacc
    from concourse.bass_utils import run_bass_kernel_spmd

    nc = bacc.Bacc("TRN2", target_bir_lowering=False, num_devices=1)
    arrays, d = {}, {}
    for name in _INS:
        a = np.ascontiguousarray(inputs[name])
        if name == "x":
            a = a.reshape(SEQ, D_MODEL)
        arrays[f"in_{name}"] = a
    arrays["in_tables"] = constant_tables()
    for name, a in arrays.items():
        d[name[3:]] = nc.dram_tensor(name, a.shape, mybir.dt.from_np(a.dtype), kind="ExternalInput").ap()
    d["out"] = nc.dram_tensor("out", [SEQ, D_MODEL], F32, kind="ExternalOutput").ap()
    trunk(nc, d)
    r = run_bass_kernel_spmd(nc, [arrays], core_ids=[0])
    return r.results[0]["out"].reshape(1, SEQ, D_MODEL)
```

```python
import math
from contextlib import ExitStack

import concourse.bass as bass
from concourse import mybir

F32 = mybir.dt.float32
F32R = mybir.dt.float32r
I32 = mybir.dt.int32
ALU = mybir.AluOpType
ACT = mybir.ActivationFunctionType

P = 128
D_MODEL, SEQ, DEPTH = 1024, 256, 2
HEAD_DIM, ROPE_HALF = 64, 8
ROPE_THETA = 500000.0
FOX_HEADS, DIL_KV_HEADS, MOBA_HEADS = 6, 4, 6
DIL_PATTERNS = ((128, 1), (512, 4), (2048, 16))
GROUPS = len(DIL_PATTERNS)
D_FF = 2816
LN_EPS = 1e-5
ALPHA = (2 * DEPTH) ** 0.25
SCALE = HEAD_DIM ** -0.5
TT = SEQ // P
KT = D_MODEL // P
NW = 512
D_IN = 6662
GATE0 = D_IN - 3 * D_MODEL
BIG = 1e30
TOP = 3e38

QKV = [
    (0, 512, [("qk", 0, 0, 512)]),
    (512, 512, [("qk", 0, 4, 256), ("v", 0, 0, 256)]),
    (1024, 134, [("v", 0, 256, 128), ("f", 0, 0, FOX_HEADS)]),
    (1158, 512, [("qk", 1, 0, 512)]),
    (1670, 512, [("qk", 1, 4, 512)]),
    (2182, 512, [("v", 1, 0, 256), ("qk", 2, 0, 256)]),
    (2694, 512, [("qk", 2, 2, 512)]),
    (3206, 384, [("v", 2, 0, 384)]),
]
BRANCH_KT = [3, 2, 3]
BRANCH_HEADS = [FOX_HEADS, DIL_KV_HEADS, MOBA_HEADS]
K_PAIR = [3, 6, 3]
HI_SLOTS, RAW_SLOTS = 5, 3
HELD = 3
STAGES, PSLOTS = 2, 3
FFN_CHUNKS = D_FF // 256


def layer_pieces(layer, w):
    def rows(m, k0, nk, c0, width):
        return m[layer, k0 * P:(k0 + nk) * P, c0:c0 + width].rearrange("(k p) n -> p k n", p=P)

    out = {}
    order = []

    def piece(name, transfers, nk, cols):
        out[name] = (transfers, nk, cols)
        order.append(name)

    for c, (c0, width, _) in enumerate(QKV):
        for half in range(2):
            piece(("qkv", c, half), [(rows(w["w_in"], 4 * half, 4, c0, width), 0, width)], 4, width)
    for b, name in enumerate(("w_pa", "w_pb", "w_pc")):
        for n in range(2):
            for half in range(2):
                c0 = GATE0 + b * D_MODEL + n * NW
                piece(("gate", b, n, half), [(rows(w["w_in"], 4 * half, 4, c0, NW), 0, NW)], 4, NW)
        for n in range(2):
            piece(("proj", b, n), [(rows(w[name], 0, BRANCH_KT[b], n * NW, NW), 0, NW)], BRANCH_KT[b], NW)
    for half in range(2):
        for n in range(2):
            piece(("wo", half, n), [(rows(w["w_o"], 4 * half, 4, n * NW, NW), 0, NW)], 4, NW)

    def gate_up(c):
        for half in range(2):
            piece(("gu", c, half), [(rows(w["w_gate"], 4 * half, 4, c * 256, 256), 0, 256),
                                    (rows(w["w_up"], 4 * half, 4, c * 256, 256), 256, 256)], 4, NW)

    def down(c):
        piece(("down", c), [(rows(w["w_down"], 2 * c, 2, 0, D_MODEL), 0, D_MODEL)], 2, D_MODEL)

    gate_up(0)
    gate_up(1)
    down(0)
    for c in range(2, FFN_CHUNKS):
        gate_up(c)
        if c < FFN_CHUNKS - HELD + 1:
            down(c - 1)
    for c in range(FFN_CHUNKS - HELD, FFN_CHUNKS):
        down(c)
    return order, out


class Counts:

    def __init__(self):
        self.n = {}

    def next(self, key):
        self.n[key] = self.n.get(key, 0) + 1
        return self.n[key]


def write_plan(orders, base):
    plan = []
    count = Counts()
    aux = [0]
    gu_use = [0]

    def bank(b):
        return b, count.next(("bank", b))

    def aux_bank():
        aux[0] += 1
        return bank(6 + aux[0] % 2)

    def turn(src, buf, k0, nk, t, dst, dst_k0, ready):
        use = aux_bank()
        plan.append(("turn", src, buf, k0, nk, t, dst, dst_k0, use, ready, count.next("turn")))
        return use

    total = sum(len(o) for o in orders)
    split_next = [0]

    lo_waiting = []

    def split_hi():
        i = split_next[0]
        if i < total:
            plan.append(("hi", i, release.get(i - HI_SLOTS)))
            lo_waiting.append(i)
            split_next[0] += 1

    freed = [0]

    def split_lo():
        if lo_waiting:
            plan.append(("lo", lo_waiting.pop(0)))

    release = {}

    def mm(i, t, lhs, outs, frees, lhs_ready, full=()):
        while lo_waiting and lo_waiting[0] <= i:
            split_lo()
        split_lo()
        if freed[0]:
            freed[0] -= 1
            split_hi()
        plan.append(("mm", i, t, lhs, outs, frees and not full, lhs_ready, full))
        if frees:
            release[i] = ("filled", full[-1]) if full else ("used", count.next("used"))
            freed[0] += 1

    norm = [0]

    def layer_norm(t, src, times):
        norm[0] += 1
        plan.append(("norm", t, src, norm[0], times))
        return norm[0]

    turned = {}
    norm_r = {0: layer_norm(0, None, 1)}

    def turn_x(t):
        for j in range(2):
            turned[t] = turn("x", 0, 4 * j, 4, t, "act", 4 * j, ("x", norm_r[t]))

    turn_x(0)
    for _ in range(HI_SLOTS):
        split_hi()
    split_lo()
    split_lo()
    norm_r[1] = layer_norm(1, None, 1)

    staged = [0]
    events = []
    for layer, order in enumerate(orders):
        at = {name: base[layer] + n for n, name in enumerate(order)}
        g0 = 3 * layer

        units = [(b, h, t) for b in range(3) for h in range(BRANCH_HEADS[b]) for t in range(TT)]
        stage_of = {}
        tick_at = [0]

        def tick():
            k = tick_at[0]
            tick_at[0] += 1
            if 0 <= k - 2 < len(units):
                d = stage_of[k - 2]
                d["pt"] = aux_bank()
                d["last"] = k - 2 == len(units) - 1
                plan.append(("turn_p", d))
            if 0 <= k - 3 < len(units):
                d = stage_of[k - 3]
                d["o"] = aux_bank()
                plan.append(("values", d, g0 + d["b"]))
                last_y[d["b"]] = d["o"]
                if d["h"] == BRANCH_HEADS[d["b"]] - 1 and d["t"] == TT - 1:
                    pend_y.append(d["b"])
            if k < len(units):
                b, h, t = units[k]
                width = (t + 1) * P
                if b == 1:
                    s = [bank(4)] + ([bank(5)] if t else [])
                else:
                    s = [bank(4 + k % 2)]
                u = layer * len(units) + k
                stage_of[k] = dict(b=b, h=h, t=t, s=s, u=u, w=width, sum_n=count.next("sum") if b == 1 else 0)
                stage_of[k]["qk"] = qk_last[b]
                plan.append(("scores", stage_of[k], g0 + b))
                if b == 0 and t == 1 and h + 1 < FOX_HEADS:
                    plan.append(("decay", layer, h + 1, aux_bank()))

        pend_y = []
        last_y = {}
        qk_last = {}
        y_turned = {}
        later = []

        def flush_y():
            for b in list(pend_y):
                pend_y.remove(b)

                def turn_y(b=b):
                    for t in range(TT):
                        y_turned[b] = turn("y", 0, 0, BRANCH_KT[b], t, "y", 3 * ((g0 + b) % 2),
                                           ("bank", last_y[b]))
                turn_y()

        def flush():
            todo, later[:] = list(later), []
            for f in todo:
                f()

        def qkv_done(c, t, use):
            segs = []
            col = 0
            for kind, b, first, width in QKV[c][2]:
                segs.append((kind, b, first, col, width))
                col += width
            ev = None
            for kind, b, first, col, width in segs:
                if kind == "qk":
                    staged[0] += 1
                    ev = dict(e=staged[0], b=b, pair=first, np=width // P, t=t, rope=b > 0, g=g0 + b, col=col)
            plan.append(("spread", layer, c, t, use, segs, ev, g0))
            if ev is not None:
                ev["rope_n"] = count.next("rope") if ev["rope"] else 0
                ev["use"] = use
                events.append(ev)
                ev["prev"] = events[-1 - STAGES] if len(events) > STAGES else None

                def turn_qk(ev=ev):
                    ev["bank"] = aux_bank()
                    qk_last[ev["b"]] = ev["bank"]
                    plan.append(("turn_qk", ev))
                later.append(turn_qk)

        def qkv(c, t, halves, use, frees, tick_too):
            for half in halves:
                mm(at[("qkv", c, half)], t, ("act", 4 * half), [(use, 0, QKV[c][1], half == 0, half == 1)],
                   frees, turned[t], (use,) if half else ())
                if tick_too and not (half == 1):
                    flush_y()
                    if c == 3 and t == TT - 1:
                        plan.append(("forget_sum", layer, aux_bank()))
                        plan.append(("decay", layer, 0, aux_bank()))
                    if c > 3:
                        tick()
                    flush()
            if halves[-1] == 1:
                if tick_too:
                    flush_y()
                    tick()
                flush()
                qkv_done(c, t, use)

        for t in range(TT):
            for c in range(2):
                use0 = bank(2 * c + t)
                qkv(c, t, (0,), use0, t == TT - 1, False)
                if t == 0 and c == 1:
                    turn_x(1)
                qkv(c, t, (1,), use0, t == TT - 1, False)
        for c in range(2, len(QKV)):
            use = [bank(2 * (c % 2) + t) for t in range(TT)]
            for half in range(2):
                for t in range(TT):
                    qkv(c, t, (half,), use[t], t == TT - 1, c > 2)
            if c == 2:
                plan.append(("forget", layer, use[TT - 1]))

        merged_done = {}

        def gates(b):
            for n in range(2):
                use = [bank(2 * n + t) for t in range(TT)]
                for half in range(2):
                    for t in range(TT):
                        mm(at[("gate", b, n, half)], t, ("act", 4 * half), [(use[t], 0, NW, half == 0, half == 1)],
                           t == TT - 1, turned[t], (use[t],) if half else ())
                        flush_y()
                        if half:
                            plan.append(("gate", n, t, use[t], merged_done.get((n, t)) if b == 2 else None))
                        if tick_at[0] < len(units) + 3:
                            tick()
                            flush()

        def turn_merged(n, t):
            turned["m", n, t] = turn("merged", 0, 4 * n, 4, t, "act", 4 * n, ("merge", merged_done[n, t]))

        def proj(b):
            for n in range(2):
                for t in range(TT):
                    use = bank(2 * n + t)
                    mm(at[("proj", b, n)], t, ("y", 3 * ((g0 + b) % 2)), [(use, 0, NW, True, True)],
                       t == TT - 1, y_turned[b], (use,))
                    flush_y()
                    plan.append(("merge", b, n, t, use))
                    if b > 0:
                        merged_done[n, t] = count.next("merge")
                    if tick_at[0] < len(units) + 3:
                        tick()
                    if b == 2 and n == 1:
                        turn_merged(0, t)

        for b in range(3):
            gates(b)
            proj(b)

        wo_use = {}
        for t in range(TT):
            wo_use[t] = [bank(2 * n + t) for n in range(2)]
            for half in range(2):
                for n in range(2):
                    if t == 1 and half == 1 and n == 1:
                        turn_x(0)
                    mm(at[("wo", half, n)], t, ("act", 4 * half), [(wo_use[t][n], 0, NW, half == 0, half == 1)],
                       t == TT - 1, turned["m", half, t], (wo_use[t][n],) if half else ())
                    if half == 0 and n == 0 and t == 0:
                        turn_merged(1, 0)
                        turn_merged(1, 1)
            norm_r[t] = layer_norm(t, wo_use[t], 2)

        hid = {}

        def gu_bank():
            gu_use[0] += 1
            return bank(4 + gu_use[0] % 2)

        def gate_up(c, t, half, use, frees):
            mm(at[("gu", c, half)], t, ("act", 4 * half), [(use, 0, NW, half == 0, half == 1)],
               frees, turned[t], (use,) if half else ())
            if half:
                hid[c, t] = use
                plan.append(("hidden", c, t, use, count.next("hid")))

        def turn_hid(c, t):
            turned["h", c, t] = turn("hid", c % 2, 0, 2, t, "y", 2 * (c % 3), ("bank", hid[c, t]))

        down_use = {t: None for t in range(TT)}

        def down(c, t, frees):
            if c == 0:
                down_use[t] = [bank(2 * n + t) for n in range(2)]
            last = c == FFN_CHUNKS - 1
            mm(at[("down", c)], t, ("y", 2 * (c % 3)),
               [(down_use[t][n], n * NW, NW, c == 0, last) for n in range(2)],
               frees, turned["h", c, t], tuple(down_use[t]) if last else ())

        for t in range(TT):
            for c in range(2):
                use = gu_bank()
                for half in range(2):
                    if t == 0 and c == 1 and half == 1:
                        turn_x(1)
                    gate_up(c, t, half, use, t == TT - 1)
                if t or c:
                    turn_hid(*((c - 1, t) if c else (1, t - 1)))
        down(0, 0, False)
        down(0, 1, True)
        turn_hid(1, 1)
        for c in range(2, FFN_CHUNKS):
            use = [gu_bank() for _ in range(TT)]
            for t in range(TT):
                gate_up(c, t, 0, use[t], t == TT - 1)
            if c > 2:
                for t in range(TT):
                    turn_hid(c - 1, t)
            for t in range(TT):
                gate_up(c, t, 1, use[t], t == TT - 1)
            if c < FFN_CHUNKS - HELD + 1:
                for t in range(TT):
                    down(c - 1, t, t == TT - 1)
        last = FFN_CHUNKS - 1
        for t in range(TT):
            for c in range(FFN_CHUNKS - HELD, FFN_CHUNKS):
                if c == last and t == 0:
                    for tt in range(TT):
                        turn_hid(last, tt)
                if c == last and t == TT - 1 and layer < DEPTH - 1:
                    turn_x(0)
                down(c, t, t == TT - 1)
            norm_r[t] = layer_norm(t, down_use[t], 1)
    return plan


TABLE_COLS = P + SEQ + SEQ + GROUPS * SEQ + 2 * TT * ROPE_HALF


def norm_params(d, j):
    if j == 0:
        return d["ln_in_g"], d["ln_in_b"]
    layer, second = (j - 1) // 2, (j - 1) % 2
    name = "ln2" if second else "ln1"
    return d[name + "_g"][layer], d[name + "_b"][layer]


def trunk(nc, d):
    orders, pieces, base = [], [], []
    for layer in range(DEPTH):
        order, table = layer_pieces(layer, d)
        base.append(len(pieces))
        orders.append(order)
        pieces += [table[name] for name in order]
    PLAN = write_plan(orders, base)

    with ExitStack() as ctx:
        def sb(name, shape, dtype=F32):
            return ctx.enter_context(nc.sbuf_tensor(name, shape, dtype))

        def sem(name):
            return ctx.enter_context(nc.semaphore(name))

        bank = [ctx.enter_context(nc.psum_tensor(f"bank{b}", [P, 512], F32)) for b in range(8)]
        raw = [sb(f"raw{s}", [P, 2048]) for s in range(RAW_SLOTS)]
        w_hi = [sb(f"w_hi{s}", [P, 2048], F32R) for s in range(HI_SLOTS)]
        w_lo = [sb(f"w_lo{s}", [P, 2048], F32R) for s in range(HI_SLOTS)]
        x = [sb(f"x{t}", [P, D_MODEL]) for t in range(TT)]
        hi = {n: sb(n + "_hi", [P, k, SEQ], F32R) for n, k in
              (("act", KT), ("y", 6))}
        lo = {n: sb(n + "_lo", [P, k, SEQ], F32R) for n, k in
              (("act", KT), ("y", 6))}
        values = [sb(f"values{s}", [P, TT, 384]) for s in range(2)]
        qk_t = [sb(f"qk_t{s}", [P, 8, SEQ]) for s in range(2)]
        stage = [sb(f"stage{s}", [P, 512]) for s in range(STAGES)]
        shared = sb("shared", [P, PSLOTS * GROUPS * SEQ])
        prob = [shared[:, s * GROUPS * SEQ:(s + 1) * GROUPS * SEQ] for s in range(PSLOTS)]
        gain_bias = shared[:, 0:2 * D_MODEL].rearrange("p (a n) -> p a n", a=2)
        prob_t = [sb(f"prob_t{s}", [P, SEQ]) for s in range(2)]
        y = sb("y", [P, TT, 384])
        act_fn = [sb(f"act_fn{s}", [P, 512]) for s in range(4)]
        merged = [sb(f"merged{t}", [P, D_MODEL]) for t in range(TT)]
        tables = sb("tables", [P, TABLE_COLS])
        decay = [sb(f"decay{s}", [P, 3 * P]) for s in range(2)]
        neg_max = sb("neg_max", [P, 4])
        denom = sb("denom", [P, 4])
        rdenom = sb("rdenom", [P, 4])
        f_bias = sb("f_bias", [P, DEPTH, FOX_HEADS])
        f_in = sb("f_in", [P, TT, FOX_HEADS])
        f_neg_abs = sb("f_neg_abs", [P, TT, FOX_HEADS])
        f_exp = sb("f_exp", [P, TT, FOX_HEADS])
        neg_logf = sb("neg_logf", [P, TT, FOX_HEADS])
        logf_hi = sb("logf_hi", [P, TT, FOX_HEADS], F32R)
        logf_lo = sb("logf_lo", [P, TT, FOX_HEADS], F32R)
        upper_r = sb("upper_r", [P, SEQ], F32R)
        neg_cum = sb("neg_cum", [P, TT, FOX_HEADS])
        rope_cos = sb("rope_cos", [P, 8, 2, ROPE_HALF])
        rope_sin = sb("rope_sin", [P, 8, 2, ROPE_HALF])
        stats = sb("stats", [P, 2, 6])
        mean_var = sb("mean_var", [P, 2])
        var_eps = sb("var_eps", [P, 1])
        rstd = sb("rstd", [P, 1])
        newton = sb("newton", [P, 1])

        col = 0

        def table(width):
            nonlocal col
            col += width
            return tables[:, col - width:col]

        ident = table(P)
        upper = table(SEQ)
        causal = table(SEQ)
        dil_mask = table(GROUPS * SEQ).rearrange("p (g k) -> p g k", g=GROUPS)
        cos = table(TT * ROPE_HALF).rearrange("p (t i) -> p t i", t=TT)
        sin = table(TT * ROPE_HALF).rearrange("p (t i) -> p t i", t=TT)

        raw_full = [sem(f"raw_full{s}") for s in range(RAW_SLOTS)]
        filled = [sem(f"filled{b}") for b in range(8)]
        drained = [sem(f"drained{b}") for b in range(8)]
        hi_done = sem("hi_done")
        lo_done = sem("lo_done")
        piece_used = sem("piece_used")
        turn_hi = sem("turn_hi")
        roped = sem("roped")
        exp_done = sem("exp_done")
        summed = sem("summed")
        silu_done = sem("silu_done")
        merge_done = sem("merge_done")
        x_ready = sem("x_ready")
        x_loaded = [sem(f"x_loaded{t}") for t in range(TT)]
        gb_loaded = sem("gb_loaded")
        ident_loaded = sem("ident_loaded")
        tables_loaded = sem("tables_loaded")
        neg_abs_ready = sem("neg_abs_ready")
        log_ready = sem("log_ready")
        logf_ready = sem("logf_ready")
        logf_hi_done = sem("logf_hi_done")
        logf_lo_done = sem("logf_lo_done")
        act_own = sem("act_own")
        dve_own = sem("dve_own")
        pool_own = sem("pool_own")
        out_done = sem("out_done")

        raw_count, so_far = [], [0] * RAW_SLOTS
        for i, (transfers, _, _) in enumerate(pieces):
            so_far[i % RAW_SLOTS] += 16 * len(transfers)
            raw_count.append(so_far[i % RAW_SLOTS])

        def weights(ring, i, n_rows):
            _, nk, cols = pieces[i]
            return ring[i % n_rows][:, 0:nk * cols]

        def source(src, buf, k, t):
            if src == "x":
                return x[t][:, k * P:(k + 1) * P]
            if src == "y":
                return y[:, t, k * P:(k + 1) * P]
            if src == "merged":
                return merged[t][:, k * P:(k + 1) * P]
            return act_fn[2 * buf + t][:, 256 + k * P:256 + (k + 1) * P]

        def group_view(ap, groups, width):
            return ap[:, 0:groups * width].rearrange("p (g k) -> p g k", g=groups)

        block = ctx.enter_context(nc.Block())

        @block.sync
        def _(sp):
            def load_gain_bias(j):
                g, b = norm_params(d, j)
                if j % 2:
                    b_pt, n_pt = last_probs
                    sp.wait_ge(filled[b_pt], n_pt)
                elif j:
                    sp.wait_ge(x_ready, TT * j)
                sp.dma_start(gain_bias[:, 0, :], g.partition_broadcast(P)).then_inc(gb_loaded, 16)
                sp.dma_start(gain_bias[:, 1, :], b.partition_broadcast(P)).then_inc(gb_loaded, 16)

            last_probs = None
            sp.dma_start(x[0][:, :], d["x"][0:P, :]).then_inc(x_loaded[0], 16)
            sp.dma_start(tables[:, 0:P], d["tables"][:, 0:P]).then_inc(ident_loaded, 16)
            load_gain_bias(0)
            norms, put_off = 0, None
            for step in PLAN:
                if step[0] == "hi":
                    i = step[1]
                    transfers, nk, cols = pieces[i]
                    if i >= RAW_SLOTS:
                        sp.wait_ge(lo_done, i - RAW_SLOTS + 1)
                    dst = weights(raw, i, RAW_SLOTS).rearrange("p (k n) -> p k n", k=nk)
                    for src, c0, width in transfers:
                        sp.dma_start(dst[:, :, c0:c0 + width], src).then_inc(raw_full[i % RAW_SLOTS], 16)
                    if put_off is not None:
                        put_off -= 1
                        if put_off == 0:
                            load_gain_bias(norms // TT)
                            put_off = None
                    if i == 1:
                        sp.dma_start(x[1][:, :], d["x"][P:SEQ, :]).then_inc(x_loaded[1], 16)
                    if i == 2:
                        sp.dma_start(tables[:, P:], d["tables"][:, P:]).then_inc(tables_loaded, 16)
                        sp.dma_start(f_bias[:, :, :].rearrange("p l h -> p (l h)"),
                                     d["b_f"].rearrange("l h -> (l h)").partition_broadcast(P)
                                     ).then_inc(tables_loaded, 16)
                elif step[0] == "norm":
                    norms += 1
                    if norms % TT == 0 and (norms // TT) % 2 == 0 and norms // TT <= 2 * DEPTH:
                        put_off = RAW_SLOTS
                elif step[0] == "turn_p" and step[1]["last"]:
                    last_probs = step[1]["pt"]
                    put_off = RAW_SLOTS
            for t in range(TT):
                sp.wait_ge(x_ready, TT * 2 * DEPTH + t + 1)
                sp.dma_start(d["out"][t * P:(t + 1) * P, :], x[t][:, :]).then_inc(out_done, 16)
            sp.wait_ge(out_done, 16 * TT)

        @block.gpsimd
        def _(pool):
            own = 0

            def link(ins):
                nonlocal own
                own += 1
                ins.then_inc(pool_own, 1)
                pool.wait_ge(pool_own, own)

            pool.wait_ge(tables_loaded, 32)
            for step in PLAN:
                if step[0] == "spread" and step[6] is not None and step[6]["rope"]:
                    ev = step[6]
                    b, n = ev["use"]
                    heads = 2 * ev["np"]
                    t = ev["t"]
                    v = stage[ev["e"] % STAGES][:, 0:heads * HEAD_DIM].rearrange(
                        "p (h d) -> p h d", d=HEAD_DIM)[:, :, 0:2 * ROPE_HALF].rearrange(
                        "p h (a i) -> p h a i", a=2)
                    c4 = cos[:, t, :].unsqueeze(1).unsqueeze(1).broadcast_to([P, heads, 2, ROPE_HALF])
                    s4 = sin[:, t, :].unsqueeze(1).unsqueeze(1).broadcast_to([P, heads, 2, ROPE_HALF])
                    rc, rs = rope_cos[:, 0:heads], rope_sin[:, 0:heads]
                    pool.wait_ge(drained[b], n)
                    link(pool.tensor_tensor(rc, v, c4, ALU.mult))
                    link(pool.tensor_tensor(rs, v, s4, ALU.mult))
                    link(pool.tensor_tensor(v[:, :, 0, :], rc[:, :, 0, :], rs[:, :, 1, :], ALU.subtract))
                    pool.tensor_tensor(v[:, :, 1, :], rc[:, :, 1, :], rs[:, :, 0, :], ALU.add).then_inc(roped, 1)
                    pool.wait_ge(roped, ev["rope_n"])
                elif step[0] == "scores" and step[1]["b"] == 1:
                    u = step[1]
                    w = u["w"]
                    pr = group_view(prob[u["u"] % PSLOTS], GROUPS, w)
                    pool.wait_ge(exp_done, u["u"] + 1)
                    link(pool.tensor_tensor(pr[:, 0, :], pr[:, 0, :], pr[:, 1, :], ALU.add))
                    pool.tensor_tensor(pr[:, 0, :], pr[:, 0, :], pr[:, 2, :], ALU.add).then_inc(summed, 1)

        @block.scalar
        def _(act):
            own = 0

            def link(ins):
                nonlocal own
                own += 1
                ins.then_inc(act_own, 1)
                act.wait_ge(act_own, own)

            for step in PLAN:
                kind = step[0]
                if kind == "hi":
                    i = step[1]
                    act.wait_ge(raw_full[i % RAW_SLOTS], raw_count[i])
                    if i >= HI_SLOTS:
                        how, r = step[2]
                        if how == "filled":
                            act.wait_ge(filled[r[0]], r[1])
                        else:
                            act.wait_ge(piece_used, r)
                    act.copy(weights(w_hi, i, HI_SLOTS), weights(raw, i, RAW_SLOTS)).then_inc(hi_done, 1)
                elif kind == "turn":
                    _, src, buf, k0, nk, t, dst, dk, (b, n), _, idx = step
                    act.wait_ge(filled[b], n)
                    act.copy(hi[dst][:, dk:dk + nk, t * P:(t + 1) * P],
                             group_view(bank[b], nk, P)).then_inc(turn_hi, 1)
                elif kind == "spread":
                    _, layer, c, t, (b, n), segs, ev, g0 = step
                    act.wait_ge(filled[b], n)
                    for s, (what, br, first, col0, width) in enumerate(segs):
                        src = bank[b][:, col0:col0 + width]
                        if what == "qk":
                            if ev["prev"] is not None:
                                pb_, pn = ev["prev"]["bank"]
                                act.wait_ge(filled[pb_], pn)
                            out = stage[ev["e"] % STAGES][:, 0:width]
                        elif what == "v":
                            out = values[(g0 + br) % 2][:, t, first:first + width]
                        else:
                            out = f_in[:, t, :]
                        ins = act.copy(out, src)
                    ins.then_inc(drained[b], 1)
                elif kind == "forget":
                    _, layer, _ = step
                    act.wait_ge(neg_abs_ready, layer + 1)
                    link(act.activation(f_exp[:, :, :], f_neg_abs[:, :, :], ACT.Exp))
                    act.activation(f_exp[:, :, :], f_exp[:, :, :], ACT.Ln, bias=1.0).then_inc(log_ready, 1)
                    if layer == 0:
                        act.wait_ge(tables_loaded, 32)
                        act.copy(upper_r[:, :], upper)
                    act.wait_ge(logf_ready, layer + 1)
                    act.copy(logf_hi[:, :, :], neg_logf[:, :, :]).then_inc(logf_hi_done, 1)
                elif kind == "scores":
                    u = step[1]
                    b, n = u["s"][-1]
                    slot = u["u"] % 4
                    pr = prob[u["u"] % PSLOTS][:, 0:(GROUPS if u["b"] == 1 else 1) * u["w"]]
                    act.wait_ge(drained[b], n)
                    act.activation(pr, pr, ACT.Exp, bias=neg_max[:, slot:slot + 1], scale=-1.0,
                                   accum_out=denom[:, slot:slot + 1]).then_inc(exp_done, 1)
                elif kind == "turn_p":
                    u = step[1]
                    b, n = u["pt"]
                    act.wait_ge(filled[b], n)
                    act.copy(prob_t[u["u"] % 2][:, 0:u["w"]], bank[b][:, 0:u["w"]]).then_inc(drained[b], 1)
                elif kind == "gate":
                    _, nh, t, (b, n), last_merge = step
                    act.wait_ge(filled[b], n)
                    if last_merge is not None:
                        act.wait_ge(merge_done, last_merge)
                    act.activation(act_fn[2 * nh + t][:, :], bank[b][:, :], ACT.Tanh, scale=0.5).then_inc(drained[b], 1)
                elif kind == "hidden":
                    _, c, t, (b, n), _ = step
                    act.wait_ge(filled[b], n)
                    act.activation(act_fn[2 * (c % 2) + t][:, 0:256], bank[b][:, 0:256],
                                   ACT.Silu).then_inc(silu_done, 1)

        @block.vector
        def _(dve):
            own = 0

            def link(ins):
                nonlocal own
                own += 1
                ins.then_inc(dve_own, 1)
                dve.wait_ge(dve_own, own)

            for step in PLAN:
                kind = step[0]
                if kind == "lo":
                    i = step[1]
                    dve.wait_ge(hi_done, i + 1)
                    dve.tensor_tensor(weights(w_lo, i, HI_SLOTS), weights(raw, i, RAW_SLOTS),
                                      weights(w_hi, i, HI_SLOTS).bitcast(F32), ALU.subtract).then_inc(lo_done, 1)
                elif kind == "turn":
                    _, src, buf, k0, nk, t, dst, dk, (b, n), _, idx = step
                    dve.wait_ge(turn_hi, idx)
                    dve.tensor_tensor(lo[dst][:, dk:dk + nk, t * P:(t + 1) * P], group_view(bank[b], nk, P),
                                      hi[dst][:, dk:dk + nk, t * P:(t + 1) * P].bitcast(F32),
                                      ALU.subtract).then_inc(drained[b], 1)
                elif kind == "turn_qk":
                    ev = step[1]
                    b, n = ev["bank"]
                    dve.wait_ge(filled[b], n)
                    dve.tensor_copy(qk_t[ev["g"] % 2][:, ev["pair"]:ev["pair"] + ev["np"],
                                                      ev["t"] * P:(ev["t"] + 1) * P],
                                    group_view(bank[b], ev["np"], P)).then_inc(drained[b], 1)
                elif kind == "forget":
                    _, layer, (fb, fn) = step
                    dve.wait_ge(tables_loaded, 32)
                    dve.wait_ge(drained[fb], fn)
                    link(dve.tensor_tensor(f_in[:, :, :], f_in[:, :, :],
                                           f_bias[:, layer, :].unsqueeze(1).broadcast_to([P, TT, FOX_HEADS]),
                                           ALU.add))
                    dve.scalar_tensor_tensor(out=f_neg_abs[:, :, :], in0=f_in[:, :, :], scalar=-1.0, in1=f_in[:, :, :],
                                             op0=ALU.mult, op1=ALU.min).then_inc(neg_abs_ready, 1)
                    dve.wait_ge(log_ready, layer + 1)
                    link(dve.scalar_tensor_tensor(out=neg_logf[:, :, :], in0=f_in[:, :, :], scalar=0.0,
                                                  in1=f_exp[:, :, :], op0=ALU.min, op1=ALU.subtract))
                    dve.tensor_scalar(neg_logf[:, :, :], neg_logf[:, :, :], -1.0 / SCALE, None,
                                      ALU.mult).then_inc(logf_ready, 1)
                    dve.wait_ge(logf_hi_done, layer + 1)
                    dve.tensor_tensor(logf_lo[:, :, :], neg_logf[:, :, :], logf_hi[:, :, :].bitcast(F32),
                                      ALU.subtract).then_inc(logf_lo_done, 1)
                elif kind == "forget_sum":
                    _, layer, (b, n) = step
                    dve.wait_ge(filled[b], n)
                    dve.tensor_copy(neg_cum[:, :, :], group_view(bank[b], TT, FOX_HEADS)).then_inc(drained[b], 1)
                    dve.wait_ge(drained[b], n)
                elif kind == "decay":
                    _, layer, h, (b, n) = step
                    dve.wait_ge(filled[b], n)
                    dk = decay[h % 2]
                    link(dve.scalar_tensor_tensor(out=dk[:, 0:P], in0=bank[b][:, 0:P],
                                                  scalar=neg_cum[:, 0, h:h + 1], in1=causal[:, P:SEQ],
                                                  op0=ALU.subtract, op1=ALU.add))
                    dve.scalar_tensor_tensor(out=dk[:, P:3 * P], in0=bank[b][:, 0:SEQ],
                                             scalar=neg_cum[:, 1, h:h + 1], in1=causal,
                                             op0=ALU.subtract, op1=ALU.add).then_inc(drained[b], 1)
                    dve.wait_ge(drained[b], n)
                elif kind == "scores":
                    u = step[1]
                    t, w, slot = u["t"], u["w"], u["u"] % 4
                    pr = prob[u["u"] % PSLOTS]
                    nm = neg_max[:, slot:slot + 1]
                    k0 = SEQ - w
                    if u["b"] == 1:
                        first = GROUPS if t == 0 else 2
                        b, n = u["s"][0]
                        pv = group_view(pr, GROUPS, w)
                        dve.wait_ge(filled[b], n)
                        dve.tensor_tensor_reduce(pv[:, 0:first, :], group_view(bank[b], first, w),
                                                 dil_mask[:, 0:first, k0:SEQ], -SCALE, TOP, ALU.add, ALU.min,
                                                 nm).then_inc(drained[b], 1)
                        if t:
                            dve.wait_ge(drained[b], n)
                            b, n = u["s"][1]
                            dve.wait_ge(filled[b], n)
                            dve.tensor_tensor_reduce(pv[:, 2, :], bank[b][:, 0:w], dil_mask[:, 2, k0:SEQ],
                                                     -SCALE, nm, ALU.add, ALU.min, nm).then_inc(drained[b], 1)
                    else:
                        b, n = u["s"][0]
                        if u["b"] == 0:
                            mask = decay[u["h"] % 2][:, 0:P] if t == 0 else decay[u["h"] % 2][:, P:3 * P]
                        else:
                            mask = causal[:, k0:SEQ]
                        dve.wait_ge(filled[b], n)
                        dve.tensor_tensor_reduce(pr[:, 0:w], bank[b][:, 0:w], mask, -SCALE, TOP, ALU.add,
                                                 ALU.min, nm).then_inc(drained[b], 1)
                elif kind == "values":
                    u = step[1]
                    b, n = u["o"]
                    slot = u["u"] % 4
                    dve.wait_ge(filled[b], n)
                    link(dve.reciprocal(rdenom[:, slot:slot + 1], denom[:, slot:slot + 1]))
                    dve.tensor_scalar(y[:, u["t"], u["h"] * HEAD_DIM:(u["h"] + 1) * HEAD_DIM],
                                      bank[b][:, 0:HEAD_DIM], rdenom[:, slot:slot + 1], None,
                                      ALU.mult).then_inc(drained[b], 1)
                elif kind == "merge":
                    _, br, nh, t, (b, n) = step
                    dve.wait_ge(filled[b], n)
                    out = merged[t][:, nh * NW:(nh + 1) * NW]
                    sig = act_fn[2 * nh + t][:, :]
                    if br == 0:
                        dve.scalar_tensor_tensor(out=out, in0=sig, scalar=1.0, in1=bank[b][:, :],
                                                 op0=ALU.add, op1=ALU.mult).then_inc(drained[b], 1)
                    else:
                        dve.scalar_tensor_tensor(out=sig, in0=sig, scalar=1.0, in1=bank[b][:, :],
                                                 op0=ALU.add, op1=ALU.mult).then_inc(drained[b], 1)
                        dve.wait_ge(drained[b], n)
                        dve.tensor_tensor(out, out, sig, ALU.add).then_inc(merge_done, 1)
                elif kind == "hidden":
                    _, c, t, (b, n), idx = step
                    dve.wait_ge(silu_done, idx)
                    a = act_fn[2 * (c % 2) + t]
                    dve.tensor_tensor(a[:, 256:512], a[:, 0:256], bank[b][:, 256:512],
                                      ALU.mult).then_inc(drained[b], 1)
                elif kind == "norm":
                    _, t, src, idx, times = step
                    xt = x[t]
                    if src is None:
                        dve.wait_ge(x_loaded[t], 16)
                    for nh in range(2):
                        xh = xt[:, nh * NW:(nh + 1) * NW]
                        if src is not None:
                            b, n = src[nh]
                            dve.wait_ge(filled[b], n)
                            dve.scalar_tensor_tensor(out=xh, in0=xh, scalar=times * ALPHA, in1=bank[b][:, :],
                                                     op0=ALU.mult, op1=ALU.add).then_inc(drained[b], 1)
                            dve.wait_ge(drained[b], n)
                        link(dve.bn_stats(stats[:, nh, :], xh))
                    link(dve.bn_aggr(mean_var[:, :], stats[:, :, :]))
                    link(dve.tensor_scalar(var_eps[:, :], mean_var[:, 1:2], times * times * LN_EPS, None, ALU.add))
                    link(dve.tensor_scalar(rstd[:, :].bitcast(I32), var_eps[:, :].bitcast(I32), -0.5,
                                           float(0x5F3759DF), ALU.mult, ALU.add))
                    link(dve.tensor_scalar(var_eps[:, :], var_eps[:, :], -0.5, None, ALU.mult))
                    for _ in range(3):
                        link(dve.scalar_tensor_tensor(out=newton[:, :], in0=rstd[:, :], scalar=var_eps[:, 0:1],
                                                      in1=rstd[:, :], op0=ALU.mult, op1=ALU.mult))
                        link(dve.scalar_tensor_tensor(out=rstd[:, :], in0=newton[:, :], scalar=1.5,
                                                      in1=rstd[:, :], op0=ALU.add, op1=ALU.mult))
                    dve.wait_ge(gb_loaded, 32 * ((idx + 1) // TT))
                    link(dve.scalar_tensor_tensor(out=xt[:, :], in0=xt[:, :], scalar=mean_var[:, 0:1],
                                                  in1=gain_bias[:, 0, :], op0=ALU.subtract, op1=ALU.mult))
                    dve.scalar_tensor_tensor(out=xt[:, :], in0=xt[:, :], scalar=rstd[:, 0:1],
                                             in1=gain_bias[:, 1, :], op0=ALU.mult,
                                             op1=ALU.add).then_inc(x_ready, 1)
                    dve.wait_ge(x_ready, idx)

        @block.tensor
        def _(pe):
            def take(use):
                b, n = use
                if n > 1:
                    pe.wait_ge(drained[b], n - 1)
                return bank[b], filled[b]

            pe.wait_ge(ident_loaded, 16)
            for step in PLAN:
                kind = step[0]
                if kind == "mm":
                    _, i, t, (lhs, k0), outs, frees, (lb, ln), full = step
                    _, nk, cols = pieces[i]
                    pe.wait_ge(drained[lb], ln)
                    pe.wait_ge(lo_done, i + 1)
                    wh = weights(w_hi, i, HI_SLOTS).rearrange("p (k n) -> p k n", k=nk)
                    wl = weights(w_lo, i, HI_SLOTS).rearrange("p (k n) -> p k n", k=nk)
                    for use, _, _, start, _ in outs:
                        if start:
                            take(use)
                    for o, (use, c0, width, start, stop) in enumerate(outs):
                        for k in range(nk):
                            xh = hi[lhs][:, k0 + k, t * P:(t + 1) * P]
                            xl = lo[lhs][:, k0 + k, t * P:(t + 1) * P]
                            for p, (a, w) in enumerate(((xh, wh), (xh, wl), (xl, wh))):
                                ins = pe.matmul(bank[use[0]][:, 0:width], a, w[:, k, c0:c0 + width],
                                                start=start and k == 0 and p == 0,
                                                stop=stop and k == nk - 1 and p == 2)
                        if use in full:
                            ins.then_inc(filled[use[0]], 1)
                    if frees:
                        ins.then_inc(piece_used, 1)
                elif kind == "turn":
                    _, src, buf, k0, nk, t, dst, dk, use, (what, r), idx = step
                    if what == "bank":
                        pe.wait_ge(drained[r[0]], r[1])
                    else:
                        pe.wait_ge({"x": x_ready, "merge": merge_done}[what], r)
                    out, done = take(use)
                    for k in range(nk):
                        ins = pe.transpose(out[:, k * P:(k + 1) * P], source(src, buf, k0 + k, t), ident)
                    ins.then_inc(done, 1)
                elif kind == "turn_qk":
                    ev = step[1]
                    if ev["rope"]:
                        pe.wait_ge(roped, ev["rope_n"])
                    else:
                        pe.wait_ge(drained[ev["use"][0]], ev["use"][1])
                    out, done = take(ev["bank"])
                    for k in range(ev["np"]):
                        ins = pe.transpose(out[:, k * P:(k + 1) * P],
                                           stage[ev["e"] % STAGES][:, k * P:(k + 1) * P], ident)
                    ins.then_inc(done, 1)
                elif kind == "forget_sum":
                    _, layer, use = step
                    pe.wait_ge(logf_lo_done, layer + 1)
                    out, done = take(use)
                    pe.matmul(out[:, 0:FOX_HEADS], upper[:, 0:P], neg_logf[:, 0, :], start=True, stop=True)
                    pe.matmul(out[:, FOX_HEADS:2 * FOX_HEADS], upper[:, P:SEQ], neg_logf[:, 0, :],
                              start=True, stop=False)
                    pe.matmul(out[:, FOX_HEADS:2 * FOX_HEADS], upper[:, 0:P], neg_logf[:, 1, :],
                              start=False, stop=True).then_inc(done, 1)
                elif kind == "decay":
                    _, layer, h, use = step
                    out, done = take(use)
                    for p, part in enumerate((logf_hi, logf_lo)):
                        pe.matmul(out[:, 0:SEQ], part[:, 0, h:h + 1].broadcast_to([P, P]), upper_r[:, :],
                                  start=p == 0, stop=False)
                    for p, part in enumerate((logf_hi, logf_lo)):
                        ins = pe.matmul(out[:, P:SEQ], part[:, 1, h:h + 1].broadcast_to([P, P]),
                                        upper_r[:, 0:P], start=False, stop=p == 1)
                    ins.then_inc(done, 1)
                elif kind == "scores":
                    _, u, g = step
                    br, h, t, w = u["b"], u["h"], u["t"], u["w"]
                    qb, qn = u["qk"]
                    pe.wait_ge(drained[qb], qn)
                    at = (h % 2) * HEAD_DIM
                    keys = qk_t[g % 2][at:at + HEAD_DIM, K_PAIR[br] + h // 2, 0:w]
                    for gi in range(GROUPS if br == 1 else 1):
                        q = h + gi * DIL_KV_HEADS
                        use = u["s"][1] if gi == 2 and t else u["s"][0]
                        if gi == 0 or (gi == 2 and t):
                            take(use)
                            off = 0
                        queries = qk_t[g % 2][at:at + HEAD_DIM, q // 2, t * P:(t + 1) * P]
                        ins = pe.matmul(bank[use[0]][:, off:off + w], queries, keys, start=True, stop=True)
                        off += w
                        if br != 1 or gi == 2 or (gi == 1 and t):
                            ins.then_inc(filled[use[0]], 1)
                elif kind == "turn_p":
                    u = step[1]
                    if u["b"] == 1:
                        pe.wait_ge(summed, u["sum_n"])
                    else:
                        pe.wait_ge(exp_done, u["u"] + 1)
                    out, done = take(u["pt"])
                    for j in range(u["t"] + 1):
                        ins = pe.transpose(out[:, j * P:(j + 1) * P],
                                           prob[u["u"] % PSLOTS][:, j * P:(j + 1) * P], ident)
                    ins.then_inc(done, 1)
                elif kind == "values":
                    _, u, g = step
                    pb_, pn = u["pt"]
                    pe.wait_ge(drained[pb_], pn)
                    out, done = take(u["o"])
                    h = u["h"]
                    for j in range(u["t"] + 1):
                        ins = pe.matmul(out[:, 0:HEAD_DIM], prob_t[u["u"] % 2][:, j * P:(j + 1) * P],
                                        values[g % 2][:, j, h * HEAD_DIM:(h + 1) * HEAD_DIM],
                                        start=j == 0, stop=j == u["t"])
                    ins.then_inc(done, 1)


def constant_tables():
    import numpy as np

    row = np.arange(P)[:, None]
    col = np.arange(SEQ)[None, :]
    f32 = np.float32
    ident = np.eye(P, dtype=f32)
    upper = np.where(row <= col, 1.0, 0.0).astype(f32)
    back = row + P - col
    causal = np.where(back >= 0, 0.0, -BIG).astype(f32)
    dil = [np.where((back >= 0) & (back % dil == 0) & (back // dil <= window // dil), 0.0, -BIG).astype(f32)
           for window, dil in DIL_PATTERNS]
    freq = np.power(f32(ROPE_THETA), -np.arange(ROPE_HALF, dtype=f32) * f32(2.0) / f32(2 * ROPE_HALF)).astype(f32)
    angle = [(np.arange(t * P, (t + 1) * P, dtype=f32)[:, None] * freq[None, :]).astype(f32) for t in range(TT)]
    parts = [ident, upper, causal, *dil, *[np.cos(a) for a in angle], *[np.sin(a) for a in angle]]
    return np.ascontiguousarray(np.concatenate(parts, axis=1).astype(f32))


_INS = ["x", "ln_in_g", "ln_in_b", "w_in", "b_f", "w_pa", "w_pb", "w_pc", "w_o", "ln1_g", "ln1_b",
        "w_gate", "w_up", "w_down", "ln2_g", "ln2_b"]


def kernel(**inputs):
    import numpy as np
    import concourse.bacc as bacc
    from concourse.bass_utils import run_bass_kernel_spmd

    nc = bacc.Bacc("TRN2", target_bir_lowering=False, num_devices=1)
    arrays, d = {}, {}
    for name in _INS:
        a = np.ascontiguousarray(inputs[name])
        if name == "x":
            a = a.reshape(SEQ, D_MODEL)
        arrays[f"in_{name}"] = a
    arrays["in_tables"] = constant_tables()
    for name, a in arrays.items():
        d[name[3:]] = nc.dram_tensor(name, a.shape, mybir.dt.from_np(a.dtype), kind="ExternalInput").ap()
    d["out"] = nc.dram_tensor("out", [SEQ, D_MODEL], F32, kind="ExternalOutput").ap()
    trunk(nc, d)
    r = run_bass_kernel_spmd(nc, [arrays], core_ids=[0])
    return r.results[0]["out"].reshape(1, SEQ, D_MODEL)
```

```python
import math
from contextlib import ExitStack

import concourse.bass as bass
from concourse import mybir

F32 = mybir.dt.float32
F32R = mybir.dt.float32r
I32 = mybir.dt.int32
ALU = mybir.AluOpType
ACT = mybir.ActivationFunctionType

P = 128
D_MODEL, SEQ, DEPTH = 1024, 256, 2
HEAD_DIM, ROPE_HALF = 64, 8
ROPE_THETA = 500000.0
FOX_HEADS, DIL_KV_HEADS, MOBA_HEADS = 6, 4, 6
DIL_PATTERNS = ((128, 1), (512, 4), (2048, 16))
GROUPS = len(DIL_PATTERNS)
D_FF = 2816
LN_EPS = 1e-5
ALPHA = (2 * DEPTH) ** 0.25
SCALE = HEAD_DIM ** -0.5
TT = SEQ // P
KT = D_MODEL // P
NW = 512
D_IN = 6662
GATE0 = D_IN - 3 * D_MODEL
BIG = 1e30
TOP = 3e38

QKV = [
    (0, 512, [("qk", 0, 0, 512)]),
    (512, 512, [("qk", 0, 4, 256), ("v", 0, 0, 256)]),
    (1024, 134, [("v", 0, 256, 128), ("f", 0, 0, FOX_HEADS)]),
    (1158, 512, [("qk", 1, 0, 512)]),
    (1670, 512, [("qk", 1, 4, 512)]),
    (2182, 512, [("v", 1, 0, 256), ("qk", 2, 0, 256)]),
    (2694, 512, [("qk", 2, 2, 512)]),
    (3206, 384, [("v", 2, 0, 384)]),
]
BRANCH_KT = [3, 2, 3]
BRANCH_HEADS = [FOX_HEADS, DIL_KV_HEADS, MOBA_HEADS]
K_PAIR = [3, 6, 3]
HI_SLOTS, RAW_SLOTS = 5, 3
HELD = 3
STAGES, PSLOTS = 2, 3
FFN_CHUNKS = D_FF // 256


def layer_pieces(layer, w):
    def rows(m, k0, nk, c0, width):
        return m[layer, k0 * P:(k0 + nk) * P, c0:c0 + width].rearrange("(k p) n -> p k n", p=P)

    out = {}
    order = []

    def piece(name, transfers, nk, cols):
        out[name] = (transfers, nk, cols)
        order.append(name)

    for c, (c0, width, _) in enumerate(QKV):
        for half in range(2):
            piece(("qkv", c, half), [(rows(w["w_in"], 4 * half, 4, c0, width), 0, width)], 4, width)
    for b, name in enumerate(("w_pa", "w_pb", "w_pc")):
        for n in range(2):
            for half in range(2):
                c0 = GATE0 + b * D_MODEL + n * NW
                piece(("gate", b, n, half), [(rows(w["w_in"], 4 * half, 4, c0, NW), 0, NW)], 4, NW)
        for n in range(2):
            piece(("proj", b, n), [(rows(w[name], 0, BRANCH_KT[b], n * NW, NW), 0, NW)], BRANCH_KT[b], NW)
    for half in range(2):
        for n in range(2):
            piece(("wo", half, n), [(rows(w["w_o"], 4 * half, 4, n * NW, NW), 0, NW)], 4, NW)

    def gate_up(c):
        for half in range(2):
            piece(("gu", c, half), [(rows(w["w_gate"], 4 * half, 4, c * 256, 256), 0, 256),
                                    (rows(w["w_up"], 4 * half, 4, c * 256, 256), 256, 256)], 4, NW)

    def down(c):
        piece(("down", c), [(rows(w["w_down"], 2 * c, 2, 0, D_MODEL), 0, D_MODEL)], 2, D_MODEL)

    gate_up(0)
    gate_up(1)
    down(0)
    for c in range(2, FFN_CHUNKS):
        gate_up(c)
        if c < FFN_CHUNKS - HELD + 1:
            down(c - 1)
    for c in range(FFN_CHUNKS - HELD, FFN_CHUNKS):
        down(c)
    return order, out


class Counts:

    def __init__(self):
        self.n = {}

    def next(self, key):
        self.n[key] = self.n.get(key, 0) + 1
        return self.n[key]


def write_plan(orders, base):
    plan = []
    count = Counts()
    aux = [0]
    gu_use = [0]

    def bank(b):
        return b, count.next(("bank", b))

    def aux_bank():
        aux[0] += 1
        return bank(6 + aux[0] % 2)

    def turn(src, buf, k0, nk, t, dst, dst_k0, ready):
        use = aux_bank()
        plan.append(("turn", src, buf, k0, nk, t, dst, dst_k0, use, ready, count.next("turn")))
        return use

    total = sum(len(o) for o in orders)
    split_next = [0]
    lo_waiting = []

    def split_hi():
        i = split_next[0]
        if i < total:
            plan.append(("hi", i, release.get(i - HI_SLOTS)))
            lo_waiting.append(i)
            split_next[0] += 1

    freed = [0]

    def split_lo():
        if lo_waiting:
            plan.append(("lo", lo_waiting.pop(0)))

    release = {}

    def mm(i, t, lhs, outs, frees, lhs_ready, full=()):
        while lo_waiting and lo_waiting[0] <= i:
            split_lo()
        split_lo()
        if freed[0]:
            freed[0] -= 1
            split_hi()
        plan.append(("mm", i, t, lhs, outs, frees and not full, lhs_ready, full))
        if frees:
            release[i] = ("filled", full[-1]) if full else ("used", count.next("used"))
            freed[0] += 1

    norm = [0]

    def statistics(srcs, times):
        plan.append(("statistics", list(srcs.items()), times))

    def scale(t):
        norm[0] += 1
        norm_n[t] = norm[0]
        plan.append(("scale", t, norm[0]))

    def layer_norm(t, src, times):
        statistics({t: src}, times)
        if t:
            while lo_waiting:
                split_lo()
        scale(t)

    turned = {}
    norm_n = {}

    def turn_x(t, *halves):
        for j in halves:
            turned[t, j] = turn("x", 0, 4 * j, 4, t, "act", 4 * j, ("x", 2 * (norm_n[t] - 1) + j + 1))

    def turn_second(done, halves_at=(3, 4)):
        for j in range(2):
            if halves_at[j] == done:
                turn_x(1, j)

    statistics({t: None for t in range(TT)}, 1)
    scale(0)
    split_hi()
    split_lo()
    turn_x(0, 0, 1)
    split_hi()
    split_lo()
    scale(1)
    for _ in range(HI_SLOTS - 2):
        split_hi()

    staged = [0]
    events = []
    for layer, order in enumerate(orders):
        at = {name: base[layer] + n for n, name in enumerate(order)}
        g0 = 3 * layer

        units = [(b, h, t) for b in range(3) for h in range(BRANCH_HEADS[b]) for t in range(TT)]
        stage_of = {}
        tick_at = [0]

        def tick():
            k = tick_at[0]
            tick_at[0] += 1
            if 0 <= k - 1 < len(units) and stage_of[k - 1]["b"] == 1:
                plan.append(("sum", stage_of[k - 1]))
            if 0 <= k - 2 < len(units):
                d = stage_of[k - 2]
                d["pt"] = aux_bank()
                d["last"] = k - 2 == len(units) - 1
                plan.append(("turn_p", d))
            if 0 <= k - 3 < len(units):
                d = stage_of[k - 3]
                d["o"] = aux_bank()
                plan.append(("values", d, g0 + d["b"]))
                if d["h"] == BRANCH_HEADS[d["b"]] - 1:
                    last_y[d["b"], d["t"]] = d["o"]
                    y_due.append((d["b"], d["t"]))
            if k < len(units):
                b, h, t = units[k]
                width = (t + 1) * P
                if b == 1:
                    s = [bank(4)] + ([bank(5)] if t else [])
                else:
                    s = [bank(4 + k % 2)]
                u = layer * len(units) + k
                stage_of[k] = dict(b=b, h=h, t=t, s=s, u=u, w=width, sum_n=count.next("sum") if b == 1 else 0)
                stage_of[k]["qk"] = qk_last[b]
                plan.append(("scores", stage_of[k], g0 + b))
                if b == 0 and t == 1 and h + 1 < FOX_HEADS:
                    plan.append(("decay", layer, h + 1, aux_bank()))

        y_due = []
        last_y = {}
        qk_last = {}
        y_turned = {}
        later = []

        def attend():
            due = y_due[:1]
            del y_due[:1]
            if tick_at[0] < len(units) + 3:
                tick()
            for b, t in due:
                y_turned[b, t] = turn("y", 0, 0, BRANCH_KT[b], t, "y", 3 * ((g0 + b) % 2),
                                      ("bank", last_y[b, t]))

        def flush():
            todo, later[:] = list(later), []
            for f in todo:
                f()

        def qkv_done(c, t, use):
            segs = []
            col = 0
            for kind, b, first, width in QKV[c][2]:
                segs.append((kind, b, first, col, width))
                col += width
            ev = None
            for kind, b, first, col, width in segs:
                if kind == "qk":
                    staged[0] += 1
                    ev = dict(e=staged[0], b=b, pair=first, np=width // P, t=t, rope=b > 0, g=g0 + b, col=col)
            plan.append(("spread", layer, c, t, use, segs, ev, g0))
            if ev is not None:
                ev["rope_n"] = count.next("rope") if ev["rope"] else 0
                ev["use"] = use
                events.append(ev)
                ev["prev"] = events[-1 - STAGES] if len(events) > STAGES else None

                def turn_qk(ev=ev):
                    ev["bank"] = aux_bank()
                    qk_last[ev["b"]] = ev["bank"]
                    plan.append(("turn_qk", ev))
                later.append(turn_qk)

        def qkv(c, t, half, use):
            mm(at[("qkv", c, half)], t, ("act", 4 * half), [(use, 0, QKV[c][1], half == 0, half == 1)],
               t == TT - 1, turned[t, half], (use,) if half else ())
            if (c, half, t) == (3, 0, TT - 1):
                plan.append(("forget_sum", layer, aux_bank()))
                plan.append(("decay", layer, 0, aux_bank()))
            if 2 * c + half > 6:
                attend()
            if half or c > 2:
                flush()
            if half:
                qkv_done(c, t, use)

        turn_at = (3, 4) if layer else (2, 2)
        for t in range(TT):
            for c in range(2):
                use0 = bank(2 * c + t)
                for half in range(2):
                    if t == 0:
                        turn_second(2 * c + half, turn_at)
                    qkv(c, t, half, use0)
            if t == 0:
                turn_second(4, turn_at)
        for c in range(2, len(QKV)):
            use = [bank(2 * (c % 2) + t) for t in range(TT)]
            for half in range(2):
                for t in range(TT):
                    qkv(c, t, half, use[t])
            if c == 2:
                plan.append(("forget", layer, use[TT - 1]))

        merged_done = {}

        def gates(b):
            for n in range(2):
                use = [bank(2 * n + t) for t in range(TT)]
                for half in range(2):
                    for t in range(TT):
                        mm(at[("gate", b, n, half)], t, ("act", 4 * half), [(use[t], 0, NW, half == 0, half == 1)],
                           t == TT - 1, turned[t, half], (use[t],) if half else ())
                        if half:
                            plan.append(("gate", n, t, use[t], merged_done.get((n, t)) if b == 2 else None))
                        attend()
                        flush()

        def turn_merged(n, t):
            turned["m", n, t] = turn("merged", 0, 4 * n, 4, t, "act", 4 * n, ("merge", merged_done[n, t]))

        def proj(b):
            for n in range(2):
                for t in range(TT):
                    use = bank(2 * n + t)
                    if (b, n, t) == (2, 1, 0):
                        turn_merged(0, 0)
                    mm(at[("proj", b, n)], t, ("y", 3 * ((g0 + b) % 2)), [(use, 0, NW, True, True)],
                       t == TT - 1, y_turned[b, t], (use,))
                    plan.append(("merge", b, n, t, use))
                    if b > 0:
                        merged_done[n, t] = count.next("merge")
                    attend()
            if b == 2:
                turn_merged(0, 1)

        for b in range(3):
            gates(b)
            proj(b)

        wo_use = {}
        for t in range(TT):
            wo_use[t] = [bank(2 * n + t) for n in range(2)]
            for half in range(2):
                for n in range(2):
                    if t == 1 and half == 1 and n == 1:
                        turn_x(0, 0)
                    mm(at[("wo", half, n)], t, ("act", 4 * half), [(wo_use[t][n], 0, NW, half == 0, half == 1)],
                       t == TT - 1, turned["m", half, t], (wo_use[t][n],) if half else ())
                    if half == 0 and t == 0:
                        turn_merged(1, n)
            if t:
                turn_x(0, 1)
            layer_norm(t, wo_use[t], 2)

        hid = {}

        def gu_bank():
            gu_use[0] += 1
            return bank(4 + gu_use[0] % 2)

        def gate_up(c, t, half, use, frees):
            mm(at[("gu", c, half)], t, ("act", 4 * half), [(use, 0, NW, half == 0, half == 1)],
               frees, turned[t, half], (use,) if half else ())
            if half:
                hid[c, t] = use
                plan.append(("hidden", c, t, use, count.next("hid")))

        def turn_hid(c, t):
            turned["h", c, t] = turn("hid", c % 2, 0, 2, t, "y", 2 * (c % 3), ("bank", hid[c, t]))

        down_use = {t: None for t in range(TT)}

        def down(c, t, frees):
            if c == 0:
                down_use[t] = [bank(2 * n + t) for n in range(2)]
            last = c == FFN_CHUNKS - 1
            mm(at[("down", c)], t, ("y", 2 * (c % 3)),
               [(down_use[t][n], n * NW, NW, c == 0, last) for n in range(2)],
               frees, turned["h", c, t], tuple(down_use[t]) if last else ())

        for t in range(TT):
            for c in range(2):
                use = gu_bank()
                for half in range(2):
                    if t == 0:
                        turn_second(2 * c + half)
                    gate_up(c, t, half, use, t == TT - 1)
                if t or c:
                    turn_hid(*((c - 1, t) if c else (1, t - 1)))
            if t == 0:
                turn_second(4)
        down(0, 0, False)
        down(0, 1, True)
        turn_hid(1, 1)
        for c in range(2, FFN_CHUNKS):
            use = [gu_bank() for _ in range(TT)]
            for t in range(TT):
                gate_up(c, t, 0, use[t], t == TT - 1)
            if c > 2:
                for t in range(TT):
                    turn_hid(c - 1, t)
            for t in range(TT):
                gate_up(c, t, 1, use[t], t == TT - 1)
            if c < FFN_CHUNKS - HELD + 1:
                for t in range(TT):
                    down(c - 1, t, t == TT - 1)
        last = FFN_CHUNKS - 1
        for t in range(TT):
            for c in range(FFN_CHUNKS - HELD, FFN_CHUNKS):
                if t == 0 and c > last - TT:
                    turn_hid(last, c - last + TT - 1)
                if c == last and t == TT - 1 and layer < DEPTH - 1:
                    turn_x(0, 0)
                down(c, t, t == TT - 1)
            if t and layer < DEPTH - 1:
                turn_x(0, 1)
            layer_norm(t, down_use[t], 1)
    return plan


TABLE_COLS = P + SEQ + SEQ + GROUPS * SEQ + 2 * TT * ROPE_HALF


def norm_params(d, j):
    if j == 0:
        return d["ln_in_g"], d["ln_in_b"]
    layer, second = (j - 1) // 2, (j - 1) % 2
    name = "ln2" if second else "ln1"
    return d[name + "_g"][layer], d[name + "_b"][layer]


def trunk(nc, d):
    orders, pieces, base = [], [], []
    for layer in range(DEPTH):
        order, table = layer_pieces(layer, d)
        base.append(len(pieces))
        orders.append(order)
        pieces += [table[name] for name in order]
    PLAN = write_plan(orders, base)

    with ExitStack() as ctx:
        def sb(name, shape, dtype=F32):
            return ctx.enter_context(nc.sbuf_tensor(name, shape, dtype))

        def sem(name):
            return ctx.enter_context(nc.semaphore(name))

        bank = [ctx.enter_context(nc.psum_tensor(f"bank{b}", [P, 512], F32)) for b in range(8)]
        raw = [sb(f"raw{s}", [P, 2048]) for s in range(RAW_SLOTS)]
        w_hi = [sb(f"w_hi{s}", [P, 2048], F32R) for s in range(HI_SLOTS)]
        w_lo = [sb(f"w_lo{s}", [P, 2048], F32R) for s in range(HI_SLOTS)]
        x = [sb(f"x{t}", [P, D_MODEL]) for t in range(TT)]
        hi = {n: sb(n + "_hi", [P, k, SEQ], F32R) for n, k in
              (("act", KT), ("y", 6))}
        lo = {n: sb(n + "_lo", [P, k, SEQ], F32R) for n, k in
              (("act", KT), ("y", 6))}
        values = [sb(f"values{s}", [P, TT, 384]) for s in range(2)]
        qk_t = [sb(f"qk_t{s}", [P, 8, SEQ]) for s in range(2)]
        stage = [sb(f"stage{s}", [P, 512]) for s in range(STAGES)]
        shared = sb("shared", [P, PSLOTS * GROUPS * SEQ])
        prob = [shared[:, s * GROUPS * SEQ:(s + 1) * GROUPS * SEQ] for s in range(PSLOTS)]
        gain_bias = shared[:, 0:2 * D_MODEL].rearrange("p (a n) -> p a n", a=2)
        prob_t = [sb(f"prob_t{s}", [P, SEQ]) for s in range(2)]
        y = sb("y", [P, TT, 384])
        act_fn = [sb(f"act_fn{s}", [P, 512]) for s in range(4)]
        merged = [sb(f"merged{t}", [P, D_MODEL]) for t in range(TT)]
        tables = sb("tables", [P, TABLE_COLS])
        decay = [sb(f"decay{s}", [P, 3 * P]) for s in range(2)]
        neg_max = sb("neg_max", [P, 4])
        denom = sb("denom", [P, 4])
        rdenom = sb("rdenom", [P, 4])
        f_bias = sb("f_bias", [P, DEPTH, FOX_HEADS])
        f_in = sb("f_in", [P, TT, FOX_HEADS])
        f_neg_abs = sb("f_neg_abs", [P, TT, FOX_HEADS])
        f_exp = sb("f_exp", [P, TT, FOX_HEADS])
        neg_logf = sb("neg_logf", [P, TT, FOX_HEADS])
        logf_hi = sb("logf_hi", [P, TT, FOX_HEADS], F32R)
        logf_lo = sb("logf_lo", [P, TT, FOX_HEADS], F32R)
        upper_r = sb("upper_r", [P, SEQ], F32R)
        neg_cum = sb("neg_cum", [P, TT, FOX_HEADS])
        rope_cos = sb("rope_cos", [P, 8, 2, ROPE_HALF])
        rope_sin = sb("rope_sin", [P, 8, 2, ROPE_HALF])
        stats = sb("stats", [P, TT, 2, 6])
        mean_var = sb("mean_var", [P, TT, 2])
        var_eps = sb("var_eps", [P, TT])
        half_var = sb("half_var", [P, TT])
        rstd = sb("rstd", [P, TT])
        newton = sb("newton", [P, TT])

        col = 0

        def table(width):
            nonlocal col
            col += width
            return tables[:, col - width:col]

        ident = table(P)
        upper = table(SEQ)
        causal = table(SEQ)
        dil_mask = table(GROUPS * SEQ).rearrange("p (g k) -> p g k", g=GROUPS)
        cos = table(TT * ROPE_HALF).rearrange("p (t i) -> p t i", t=TT)
        sin = table(TT * ROPE_HALF).rearrange("p (t i) -> p t i", t=TT)

        raw_full = [sem(f"raw_full{s}") for s in range(RAW_SLOTS)]
        filled = [sem(f"filled{b}") for b in range(8)]
        drained = [sem(f"drained{b}") for b in range(8)]
        hi_done = sem("hi_done")
        lo_done = sem("lo_done")
        piece_used = sem("piece_used")
        turn_hi = sem("turn_hi")
        roped = sem("roped")
        exp_done = sem("exp_done")
        summed = sem("summed")
        silu_done = sem("silu_done")
        merge_done = sem("merge_done")
        x_ready = sem("x_ready")
        x_loaded = [sem(f"x_loaded{t}") for t in range(TT)]
        gb_loaded = sem("gb_loaded")
        ident_loaded = sem("ident_loaded")
        tables_loaded = sem("tables_loaded")
        neg_abs_ready = sem("neg_abs_ready")
        log_ready = sem("log_ready")
        logf_ready = sem("logf_ready")
        logf_hi_done = sem("logf_hi_done")
        logf_lo_done = sem("logf_lo_done")
        act_own = sem("act_own")
        dve_own = sem("dve_own")
        pool_own = sem("pool_own")
        out_done = sem("out_done")

        raw_count, so_far = [], [0] * RAW_SLOTS
        for i, (transfers, _, _) in enumerate(pieces):
            so_far[i % RAW_SLOTS] += 16 * len(transfers)
            raw_count.append(so_far[i % RAW_SLOTS])

        def weights(ring, i, n_rows):
            _, nk, cols = pieces[i]
            return ring[i % n_rows][:, 0:nk * cols]

        def source(src, buf, k, t):
            if src == "x":
                return x[t][:, k * P:(k + 1) * P]
            if src == "y":
                return y[:, t, k * P:(k + 1) * P]
            if src == "merged":
                return merged[t][:, k * P:(k + 1) * P]
            return act_fn[2 * buf + t][:, 256 + k * P:256 + (k + 1) * P]

        def group_view(ap, groups, width):
            return ap[:, 0:groups * width].rearrange("p (g k) -> p g k", g=groups)

        block = ctx.enter_context(nc.Block())

        @block.sync
        def _(sp):
            def load_gain_bias(j):
                g, b = norm_params(d, j)
                if j % 2:
                    b_pt, n_pt = last_probs
                    sp.wait_ge(filled[b_pt], n_pt)
                elif j:
                    sp.wait_ge(x_ready, 2 * TT * j)
                sp.dma_start(gain_bias[:, 0, :], g.partition_broadcast(P)).then_inc(gb_loaded, 16)
                sp.dma_start(gain_bias[:, 1, :], b.partition_broadcast(P)).then_inc(gb_loaded, 16)

            for t in range(TT):
                sp.dma_start(x[t][:, :], d["x"][t * P:(t + 1) * P, :]).then_inc(x_loaded[t], 16)
            sp.dma_start(tables[:, 0:P], d["tables"][:, 0:P]).then_inc(ident_loaded, 16)
            load_gain_bias(0)
            norms, put_off, last_probs = 0, None, None
            for step in PLAN:
                if step[0] == "hi":
                    i = step[1]
                    transfers, nk, cols = pieces[i]
                    if i >= RAW_SLOTS:
                        sp.wait_ge(lo_done, i - RAW_SLOTS + 1)
                    dst = weights(raw, i, RAW_SLOTS).rearrange("p (k n) -> p k n", k=nk)
                    for src, c0, width in transfers:
                        sp.dma_start(dst[:, :, c0:c0 + width], src).then_inc(raw_full[i % RAW_SLOTS], 16)
                    if put_off is not None:
                        put_off -= 1
                        if put_off == 0:
                            load_gain_bias(norms // TT)
                            put_off = None
                    if i == 2:
                        sp.dma_start(tables[:, P:], d["tables"][:, P:]).then_inc(tables_loaded, 16)
                        sp.dma_start(f_bias[:, :, :].rearrange("p l h -> p (l h)"),
                                     d["b_f"].rearrange("l h -> (l h)").partition_broadcast(P)
                                     ).then_inc(tables_loaded, 16)
                elif step[0] == "scale":
                    norms += 1
                    if norms % TT == 0 and (norms // TT) % 2 == 0 and norms // TT <= 2 * DEPTH:
                        put_off = RAW_SLOTS
                elif step[0] == "turn_p" and step[1]["last"]:
                    last_probs = step[1]["pt"]
                    put_off = RAW_SLOTS
            for t in range(TT):
                for nh in range(2):
                    sp.wait_ge(x_ready, 2 * (TT * 2 * DEPTH + t) + nh + 1)
                    sp.dma_start(d["out"][t * P:(t + 1) * P, nh * NW:(nh + 1) * NW],
                                 x[t][:, nh * NW:(nh + 1) * NW]).then_inc(out_done, 16)
            sp.wait_ge(out_done, 16 * TT * 2)

        @block.gpsimd
        def _(pool):
            own = 0

            def link(ins):
                nonlocal own
                own += 1
                ins.then_inc(pool_own, 1)
                pool.wait_ge(pool_own, own)

            pool.wait_ge(tables_loaded, 32)
            for step in PLAN:
                if step[0] == "spread" and step[6] is not None and step[6]["rope"]:
                    ev = step[6]
                    b, n = ev["use"]
                    heads = 2 * ev["np"]
                    t = ev["t"]
                    v = stage[ev["e"] % STAGES][:, 0:heads * HEAD_DIM].rearrange(
                        "p (h d) -> p h d", d=HEAD_DIM)[:, :, 0:2 * ROPE_HALF].rearrange(
                        "p h (a i) -> p h a i", a=2)
                    c4 = cos[:, t, :].unsqueeze(1).unsqueeze(1).broadcast_to([P, heads, 2, ROPE_HALF])
                    s4 = sin[:, t, :].unsqueeze(1).unsqueeze(1).broadcast_to([P, heads, 2, ROPE_HALF])
                    rc, rs = rope_cos[:, 0:heads], rope_sin[:, 0:heads]
                    pool.wait_ge(drained[b], n)
                    link(pool.tensor_tensor(rc, v, c4, ALU.mult))
                    link(pool.tensor_tensor(rs, v, s4, ALU.mult))
                    link(pool.tensor_tensor(v[:, :, 0, :], rc[:, :, 0, :], rs[:, :, 1, :], ALU.subtract))
                    pool.tensor_tensor(v[:, :, 1, :], rc[:, :, 1, :], rs[:, :, 0, :], ALU.add).then_inc(roped, 1)
                    pool.wait_ge(roped, ev["rope_n"])
                elif step[0] == "sum":
                    u = step[1]
                    w = u["w"]
                    pr = group_view(prob[u["u"] % PSLOTS], GROUPS, w)
                    pool.wait_ge(exp_done, u["u"] + 1)
                    link(pool.tensor_tensor(pr[:, 0, :], pr[:, 0, :], pr[:, 1, :], ALU.add))
                    pool.tensor_tensor(pr[:, 0, :], pr[:, 0, :], pr[:, 2, :], ALU.add).then_inc(summed, 1)

        @block.scalar
        def _(act):
            own = 0

            def link(ins):
                nonlocal own
                own += 1
                ins.then_inc(act_own, 1)
                act.wait_ge(act_own, own)

            for step in PLAN:
                kind = step[0]
                if kind == "hi":
                    i = step[1]
                    act.wait_ge(raw_full[i % RAW_SLOTS], raw_count[i])
                    if i >= HI_SLOTS:
                        how, r = step[2]
                        if how == "filled":
                            act.wait_ge(filled[r[0]], r[1])
                        else:
                            act.wait_ge(piece_used, r)
                    act.copy(weights(w_hi, i, HI_SLOTS), weights(raw, i, RAW_SLOTS)).then_inc(hi_done, 1)
                elif kind == "turn":
                    _, src, buf, k0, nk, t, dst, dk, (b, n), _, idx = step
                    act.wait_ge(filled[b], n)
                    act.copy(hi[dst][:, dk:dk + nk, t * P:(t + 1) * P],
                             group_view(bank[b], nk, P)).then_inc(turn_hi, 1)
                elif kind == "spread":
                    _, layer, c, t, (b, n), segs, ev, g0 = step
                    act.wait_ge(filled[b], n)
                    for s, (what, br, first, col0, width) in enumerate(segs):
                        src = bank[b][:, col0:col0 + width]
                        if what == "qk":
                            if ev["prev"] is not None:
                                pb_, pn = ev["prev"]["bank"]
                                act.wait_ge(filled[pb_], pn)
                            out = stage[ev["e"] % STAGES][:, 0:width]
                        elif what == "v":
                            out = values[(g0 + br) % 2][:, t, first:first + width]
                        else:
                            out = f_in[:, t, :]
                        ins = act.copy(out, src)
                    ins.then_inc(drained[b], 1)
                elif kind == "forget":
                    _, layer, _ = step
                    act.wait_ge(neg_abs_ready, layer + 1)
                    link(act.activation(f_exp[:, :, :], f_neg_abs[:, :, :], ACT.Exp))
                    act.activation(f_exp[:, :, :], f_exp[:, :, :], ACT.Ln, bias=1.0).then_inc(log_ready, 1)
                    if layer == 0:
                        act.wait_ge(tables_loaded, 32)
                        act.copy(upper_r[:, :], upper)
                    act.wait_ge(logf_ready, layer + 1)
                    act.copy(logf_hi[:, :, :], neg_logf[:, :, :]).then_inc(logf_hi_done, 1)
                elif kind == "scores":
                    u = step[1]
                    b, n = u["s"][-1]
                    slot = u["u"] % 4
                    pr = prob[u["u"] % PSLOTS][:, 0:(GROUPS if u["b"] == 1 else 1) * u["w"]]
                    act.wait_ge(drained[b], n)
                    act.activation(pr, pr, ACT.Exp, bias=neg_max[:, slot:slot + 1], scale=-1.0,
                                   accum_out=denom[:, slot:slot + 1]).then_inc(exp_done, 1)
                elif kind == "turn_p":
                    u = step[1]
                    b, n = u["pt"]
                    act.wait_ge(filled[b], n)
                    act.copy(prob_t[u["u"] % 2][:, 0:u["w"]], bank[b][:, 0:u["w"]]).then_inc(drained[b], 1)
                elif kind == "gate":
                    _, nh, t, (b, n), last_merge = step
                    act.wait_ge(filled[b], n)
                    if last_merge is not None:
                        act.wait_ge(merge_done, last_merge)
                    act.activation(act_fn[2 * nh + t][:, :], bank[b][:, :], ACT.Tanh, scale=0.5).then_inc(drained[b], 1)
                elif kind == "hidden":
                    _, c, t, (b, n), _ = step
                    act.wait_ge(filled[b], n)
                    act.activation(act_fn[2 * (c % 2) + t][:, 0:256], bank[b][:, 0:256],
                                   ACT.Silu).then_inc(silu_done, 1)

        @block.vector
        def _(dve):
            own = 0

            def mark(ins):
                nonlocal own
                own += 1
                ins.then_inc(dve_own, 1)

            def settle():
                dve.wait_ge(dve_own, own)

            def link(ins):
                mark(ins)
                settle()

            for step in PLAN:
                kind = step[0]
                if kind == "lo":
                    i = step[1]
                    dve.wait_ge(hi_done, i + 1)
                    dve.tensor_tensor(weights(w_lo, i, HI_SLOTS), weights(raw, i, RAW_SLOTS),
                                      weights(w_hi, i, HI_SLOTS).bitcast(F32), ALU.subtract).then_inc(lo_done, 1)
                elif kind == "turn":
                    _, src, buf, k0, nk, t, dst, dk, (b, n), _, idx = step
                    dve.wait_ge(turn_hi, idx)
                    dve.tensor_tensor(lo[dst][:, dk:dk + nk, t * P:(t + 1) * P], group_view(bank[b], nk, P),
                                      hi[dst][:, dk:dk + nk, t * P:(t + 1) * P].bitcast(F32),
                                      ALU.subtract).then_inc(drained[b], 1)
                elif kind == "turn_qk":
                    ev = step[1]
                    b, n = ev["bank"]
                    dve.wait_ge(filled[b], n)
                    dve.tensor_copy(qk_t[ev["g"] % 2][:, ev["pair"]:ev["pair"] + ev["np"],
                                                      ev["t"] * P:(ev["t"] + 1) * P],
                                    group_view(bank[b], ev["np"], P)).then_inc(drained[b], 1)
                elif kind == "forget":
                    _, layer, (fb, fn) = step
                    dve.wait_ge(tables_loaded, 32)
                    dve.wait_ge(drained[fb], fn)
                    link(dve.tensor_tensor(f_in[:, :, :], f_in[:, :, :],
                                           f_bias[:, layer, :].unsqueeze(1).broadcast_to([P, TT, FOX_HEADS]),
                                           ALU.add))
                    dve.scalar_tensor_tensor(out=f_neg_abs[:, :, :], in0=f_in[:, :, :], scalar=-1.0, in1=f_in[:, :, :],
                                             op0=ALU.mult, op1=ALU.min).then_inc(neg_abs_ready, 1)
                    dve.wait_ge(log_ready, layer + 1)
                    link(dve.scalar_tensor_tensor(out=neg_logf[:, :, :], in0=f_in[:, :, :], scalar=0.0,
                                                  in1=f_exp[:, :, :], op0=ALU.min, op1=ALU.subtract))
                    dve.tensor_scalar(neg_logf[:, :, :], neg_logf[:, :, :], -1.0 / SCALE, None,
                                      ALU.mult).then_inc(logf_ready, 1)
                    dve.wait_ge(logf_hi_done, layer + 1)
                    dve.tensor_tensor(logf_lo[:, :, :], neg_logf[:, :, :], logf_hi[:, :, :].bitcast(F32),
                                      ALU.subtract).then_inc(logf_lo_done, 1)
                elif kind == "forget_sum":
                    _, layer, (b, n) = step
                    dve.wait_ge(filled[b], n)
                    dve.tensor_copy(neg_cum[:, :, :], group_view(bank[b], TT, FOX_HEADS)).then_inc(drained[b], 1)
                    dve.wait_ge(drained[b], n)
                elif kind == "decay":
                    _, layer, h, (b, n) = step
                    dve.wait_ge(filled[b], n)
                    dk = decay[h % 2]
                    link(dve.scalar_tensor_tensor(out=dk[:, 0:P], in0=bank[b][:, 0:P],
                                                  scalar=neg_cum[:, 0, h:h + 1], in1=causal[:, P:SEQ],
                                                  op0=ALU.subtract, op1=ALU.add))
                    dve.scalar_tensor_tensor(out=dk[:, P:3 * P], in0=bank[b][:, 0:SEQ],
                                             scalar=neg_cum[:, 1, h:h + 1], in1=causal,
                                             op0=ALU.subtract, op1=ALU.add).then_inc(drained[b], 1)
                    dve.wait_ge(drained[b], n)
                elif kind == "scores":
                    u = step[1]
                    t, w, slot = u["t"], u["w"], u["u"] % 4
                    pr = prob[u["u"] % PSLOTS]
                    nm = neg_max[:, slot:slot + 1]
                    k0 = SEQ - w
                    if u["b"] == 1:
                        first = GROUPS if t == 0 else 2
                        b, n = u["s"][0]
                        pv = group_view(pr, GROUPS, w)
                        dve.wait_ge(filled[b], n)
                        dve.tensor_tensor_reduce(pv[:, 0:first, :], group_view(bank[b], first, w),
                                                 dil_mask[:, 0:first, k0:SEQ], -SCALE, TOP, ALU.add, ALU.min,
                                                 nm).then_inc(drained[b], 1)
                        if t:
                            dve.wait_ge(drained[b], n)
                            b, n = u["s"][1]
                            dve.wait_ge(filled[b], n)
                            dve.tensor_tensor_reduce(pv[:, 2, :], bank[b][:, 0:w], dil_mask[:, 2, k0:SEQ],
                                                     -SCALE, nm, ALU.add, ALU.min, nm).then_inc(drained[b], 1)
                    else:
                        b, n = u["s"][0]
                        if u["b"] == 0:
                            mask = decay[u["h"] % 2][:, 0:P] if t == 0 else decay[u["h"] % 2][:, P:3 * P]
                        else:
                            mask = causal[:, k0:SEQ]
                        dve.wait_ge(filled[b], n)
                        dve.tensor_tensor_reduce(pr[:, 0:w], bank[b][:, 0:w], mask, -SCALE, TOP, ALU.add,
                                                 ALU.min, nm).then_inc(drained[b], 1)
                elif kind == "values":
                    u = step[1]
                    b, n = u["o"]
                    slot = u["u"] % 4
                    dve.wait_ge(filled[b], n)
                    link(dve.reciprocal(rdenom[:, slot:slot + 1], denom[:, slot:slot + 1]))
                    dve.tensor_scalar(y[:, u["t"], u["h"] * HEAD_DIM:(u["h"] + 1) * HEAD_DIM],
                                      bank[b][:, 0:HEAD_DIM], rdenom[:, slot:slot + 1], None,
                                      ALU.mult).then_inc(drained[b], 1)
                elif kind == "merge":
                    _, br, nh, t, (b, n) = step
                    dve.wait_ge(filled[b], n)
                    out = merged[t][:, nh * NW:(nh + 1) * NW]
                    sig = act_fn[2 * nh + t][:, :]
                    if br == 0:
                        dve.scalar_tensor_tensor(out=out, in0=sig, scalar=1.0, in1=bank[b][:, :],
                                                 op0=ALU.add, op1=ALU.mult).then_inc(drained[b], 1)
                    else:
                        dve.scalar_tensor_tensor(out=sig, in0=sig, scalar=1.0, in1=bank[b][:, :],
                                                 op0=ALU.add, op1=ALU.mult).then_inc(drained[b], 1)
                        dve.wait_ge(drained[b], n)
                        dve.tensor_tensor(out, out, sig, ALU.add).then_inc(merge_done, 1)
                elif kind == "hidden":
                    _, c, t, (b, n), idx = step
                    dve.wait_ge(silu_done, idx)
                    a = act_fn[2 * (c % 2) + t]
                    dve.tensor_tensor(a[:, 256:512], a[:, 0:256], bank[b][:, 256:512],
                                      ALU.mult).then_inc(drained[b], 1)
                elif kind == "statistics":
                    _, uses, times = step
                    for t, src in uses:
                        if src is None:
                            dve.wait_ge(x_loaded[t], 16)
                        for nh in range(2):
                            xh = x[t][:, nh * NW:(nh + 1) * NW]
                            if src is not None:
                                b, n = src[nh]
                                dve.wait_ge(filled[b], n)
                                dve.scalar_tensor_tensor(out=xh, in0=xh, scalar=times * ALPHA, in1=bank[b][:, :],
                                                         op0=ALU.mult, op1=ALU.add).then_inc(drained[b], 1)
                                dve.wait_ge(drained[b], n)
                            mark(dve.bn_stats(stats[:, t, nh, :], xh))
                    settle()
                    for t, _ in uses:
                        mark(dve.bn_aggr(mean_var[:, t, :], stats[:, t, :, :]))
                    settle()
                    for t, _ in uses:
                        mark(dve.tensor_scalar(var_eps[:, t:t + 1], mean_var[:, t, 1:2], times * times * LN_EPS,
                                               None, ALU.add))
                    settle()
                    for t, _ in uses:
                        mark(dve.tensor_scalar(rstd[:, t:t + 1].bitcast(I32), var_eps[:, t:t + 1].bitcast(I32), -0.5,
                                               float(0x5F3759DF), ALU.mult, ALU.add))
                        mark(dve.tensor_scalar(half_var[:, t:t + 1], var_eps[:, t:t + 1], -0.5, None, ALU.mult))
                    settle()
                    for _ in range(3):
                        for t, _ in uses:
                            mark(dve.scalar_tensor_tensor(out=newton[:, t:t + 1], in0=rstd[:, t:t + 1],
                                                          scalar=half_var[:, t:t + 1], in1=rstd[:, t:t + 1],
                                                          op0=ALU.mult, op1=ALU.mult))
                        settle()
                        for t, _ in uses:
                            mark(dve.scalar_tensor_tensor(out=rstd[:, t:t + 1], in0=newton[:, t:t + 1], scalar=1.5,
                                                          in1=rstd[:, t:t + 1], op0=ALU.add, op1=ALU.mult))
                        settle()
                elif kind == "scale":
                    _, t, idx = step
                    dve.wait_ge(gb_loaded, 32 * ((idx + 1) // TT))
                    for nh in range(2):
                        xh = x[t][:, nh * NW:(nh + 1) * NW]
                        link(dve.scalar_tensor_tensor(out=xh, in0=xh, scalar=mean_var[:, t, 0:1],
                                                      in1=gain_bias[:, 0, nh * NW:(nh + 1) * NW],
                                                      op0=ALU.subtract, op1=ALU.mult))
                        dve.scalar_tensor_tensor(out=xh, in0=xh, scalar=rstd[:, t:t + 1],
                                                 in1=gain_bias[:, 1, nh * NW:(nh + 1) * NW], op0=ALU.mult,
                                                 op1=ALU.add).then_inc(x_ready, 1)
                    dve.wait_ge(x_ready, 2 * idx)

        @block.tensor
        def _(pe):
            def take(use):
                b, n = use
                if n > 1:
                    pe.wait_ge(drained[b], n - 1)
                return bank[b], filled[b]

            pe.wait_ge(ident_loaded, 16)
            for step in PLAN:
                kind = step[0]
                if kind == "mm":
                    _, i, t, (lhs, k0), outs, frees, (lb, ln), full = step
                    _, nk, cols = pieces[i]
                    pe.wait_ge(drained[lb], ln)
                    pe.wait_ge(lo_done, i + 1)
                    wh = weights(w_hi, i, HI_SLOTS).rearrange("p (k n) -> p k n", k=nk)
                    wl = weights(w_lo, i, HI_SLOTS).rearrange("p (k n) -> p k n", k=nk)
                    for use, _, _, start, _ in outs:
                        if start:
                            take(use)
                    for o, (use, c0, width, start, stop) in enumerate(outs):
                        for k in range(nk):
                            xh = hi[lhs][:, k0 + k, t * P:(t + 1) * P]
                            xl = lo[lhs][:, k0 + k, t * P:(t + 1) * P]
                            for p, (a, w) in enumerate(((xh, wh), (xh, wl), (xl, wh))):
                                ins = pe.matmul(bank[use[0]][:, 0:width], a, w[:, k, c0:c0 + width],
                                                start=start and k == 0 and p == 0,
                                                stop=stop and k == nk - 1 and p == 2)
                        if use in full:
                            ins.then_inc(filled[use[0]], 1)
                    if frees:
                        ins.then_inc(piece_used, 1)
                elif kind == "turn":
                    _, src, buf, k0, nk, t, dst, dk, use, (what, r), idx = step
                    if what == "bank":
                        pe.wait_ge(drained[r[0]], r[1])
                    else:
                        pe.wait_ge({"x": x_ready, "merge": merge_done}[what], r)
                    out, done = take(use)
                    for k in range(nk):
                        ins = pe.transpose(out[:, k * P:(k + 1) * P], source(src, buf, k0 + k, t), ident)
                    ins.then_inc(done, 1)
                elif kind == "turn_qk":
                    ev = step[1]
                    if ev["rope"]:
                        pe.wait_ge(roped, ev["rope_n"])
                    else:
                        pe.wait_ge(drained[ev["use"][0]], ev["use"][1])
                    out, done = take(ev["bank"])
                    for k in range(ev["np"]):
                        ins = pe.transpose(out[:, k * P:(k + 1) * P],
                                           stage[ev["e"] % STAGES][:, k * P:(k + 1) * P], ident)
                    ins.then_inc(done, 1)
                elif kind == "forget_sum":
                    _, layer, use = step
                    pe.wait_ge(logf_lo_done, layer + 1)
                    out, done = take(use)
                    pe.matmul(out[:, 0:FOX_HEADS], upper[:, 0:P], neg_logf[:, 0, :], start=True, stop=True)
                    pe.matmul(out[:, FOX_HEADS:2 * FOX_HEADS], upper[:, P:SEQ], neg_logf[:, 0, :],
                              start=True, stop=False)
                    pe.matmul(out[:, FOX_HEADS:2 * FOX_HEADS], upper[:, 0:P], neg_logf[:, 1, :],
                              start=False, stop=True).then_inc(done, 1)
                elif kind == "decay":
                    _, layer, h, use = step
                    out, done = take(use)
                    for p, part in enumerate((logf_hi, logf_lo)):
                        pe.matmul(out[:, 0:SEQ], part[:, 0, h:h + 1].broadcast_to([P, P]), upper_r[:, :],
                                  start=p == 0, stop=False)
                    for p, part in enumerate((logf_hi, logf_lo)):
                        ins = pe.matmul(out[:, P:SEQ], part[:, 1, h:h + 1].broadcast_to([P, P]),
                                        upper_r[:, 0:P], start=False, stop=p == 1)
                    ins.then_inc(done, 1)
                elif kind == "scores":
                    _, u, g = step
                    br, h, t, w = u["b"], u["h"], u["t"], u["w"]
                    qb, qn = u["qk"]
                    pe.wait_ge(drained[qb], qn)
                    at = (h % 2) * HEAD_DIM
                    keys = qk_t[g % 2][at:at + HEAD_DIM, K_PAIR[br] + h // 2, 0:w]
                    for gi in range(GROUPS if br == 1 else 1):
                        q = h + gi * DIL_KV_HEADS
                        use = u["s"][1] if gi == 2 and t else u["s"][0]
                        if gi == 0 or (gi == 2 and t):
                            take(use)
                            off = 0
                        queries = qk_t[g % 2][at:at + HEAD_DIM, q // 2, t * P:(t + 1) * P]
                        ins = pe.matmul(bank[use[0]][:, off:off + w], queries, keys, start=True, stop=True)
                        off += w
                        if br != 1 or gi == 2 or (gi == 1 and t):
                            ins.then_inc(filled[use[0]], 1)
                elif kind == "turn_p":
                    u = step[1]
                    if u["b"] == 1:
                        pe.wait_ge(summed, u["sum_n"])
                    else:
                        pe.wait_ge(exp_done, u["u"] + 1)
                    out, done = take(u["pt"])
                    for j in range(u["t"] + 1):
                        ins = pe.transpose(out[:, j * P:(j + 1) * P],
                                           prob[u["u"] % PSLOTS][:, j * P:(j + 1) * P], ident)
                    ins.then_inc(done, 1)
                elif kind == "values":
                    _, u, g = step
                    pb_, pn = u["pt"]
                    pe.wait_ge(drained[pb_], pn)
                    out, done = take(u["o"])
                    h = u["h"]
                    for j in range(u["t"] + 1):
                        ins = pe.matmul(out[:, 0:HEAD_DIM], prob_t[u["u"] % 2][:, j * P:(j + 1) * P],
                                        values[g % 2][:, j, h * HEAD_DIM:(h + 1) * HEAD_DIM],
                                        start=j == 0, stop=j == u["t"])
                    ins.then_inc(done, 1)


def constant_tables():
    import numpy as np

    row = np.arange(P)[:, None]
    col = np.arange(SEQ)[None, :]
    f32 = np.float32
    ident = np.eye(P, dtype=f32)
    upper = np.where(row <= col, 1.0, 0.0).astype(f32)
    back = row + P - col
    causal = np.where(back >= 0, 0.0, -BIG).astype(f32)
    dil = [np.where((back >= 0) & (back % dil == 0) & (back // dil <= window // dil), 0.0, -BIG).astype(f32)
           for window, dil in DIL_PATTERNS]
    freq = np.power(f32(ROPE_THETA), -np.arange(ROPE_HALF, dtype=f32) * f32(2.0) / f32(2 * ROPE_HALF)).astype(f32)
    angle = [(np.arange(t * P, (t + 1) * P, dtype=f32)[:, None] * freq[None, :]).astype(f32) for t in range(TT)]
    parts = [ident, upper, causal, *dil, *[np.cos(a) for a in angle], *[np.sin(a) for a in angle]]
    return np.ascontiguousarray(np.concatenate(parts, axis=1).astype(f32))


_INS = ["x", "ln_in_g", "ln_in_b", "w_in", "b_f", "w_pa", "w_pb", "w_pc", "w_o", "ln1_g", "ln1_b",
        "w_gate", "w_up", "w_down", "ln2_g", "ln2_b"]


def kernel(**inputs):
    import numpy as np
    import concourse.bacc as bacc
    from concourse.bass_utils import run_bass_kernel_spmd

    nc = bacc.Bacc("TRN2", target_bir_lowering=False, num_devices=1)
    arrays, d = {}, {}
    for name in _INS:
        a = np.ascontiguousarray(inputs[name])
        if name == "x":
            a = a.reshape(SEQ, D_MODEL)
        arrays[f"in_{name}"] = a
    arrays["in_tables"] = constant_tables()
    for name, a in arrays.items():
        d[name[3:]] = nc.dram_tensor(name, a.shape, mybir.dt.from_np(a.dtype), kind="ExternalInput").ap()
    d["out"] = nc.dram_tensor("out", [SEQ, D_MODEL], F32, kind="ExternalOutput").ap()
    trunk(nc, d)
    r = run_bass_kernel_spmd(nc, [arrays], core_ids=[0])
    return r.results[0]["out"].reshape(1, SEQ, D_MODEL)
```
